# Optimizing a Trainium2 kernel written in Bass

```python
import jax, jax.numpy as jnp
from jax import lax
import numpy as np

D_MODEL = 1024
BATCH = 1
SEQ = 1024
DEPTH = 2

LRU_WIDTH = D_MODEL
LRU_HEADS = 8
LRU_HEAD_DIM = LRU_WIDTH // LRU_HEADS
LRU_CONV = 4
LRU_C = 8.0
SC_WIDTH = D_MODEL
SC_HEADS = 8
SC_CONV = 3
POOL_WIDTH = 2 * D_MODEL
POOL_WINDOWS = (2, 4, 8, 16)
POOL_GROUPS = len(POOL_WINDOWS)
POOL_GROUP_DIM = POOL_WIDTH // POOL_GROUPS
EVEN_IN = 2 * LRU_WIDTH + 4 * SC_WIDTH
EVEN_SPLITS = (LRU_WIDTH, 2 * LRU_WIDTH, 2 * LRU_WIDTH + SC_WIDTH,
               2 * LRU_WIDTH + 2 * SC_WIDTH, 2 * LRU_WIDTH + 3 * SC_WIDTH)
N_EVEN = (DEPTH + 1) // 2
N_ODD = DEPTH // 2
EPS = 1e-6

kernel_name = "hybrid_rglru_shortconv_pool_adaln"

def rmsnorm(x, g):
    xf = x.astype(jnp.float32)
    y = xf * lax.rsqrt(jnp.mean(xf * xf, axis=-1, keepdims=True) + EPS)
    return (y * g.astype(jnp.float32)).astype(x.dtype)

def causal_dwconv(x, w, b=None):
    k_width = w.shape[0]
    s = x.shape[1]
    xp = jnp.pad(x, ((0, 0), (k_width - 1, 0), (0, 0)))
    y = xp[:, 0:s] * w[0]
    for k in range(1, k_width):
        y = y + xp[:, k:k + s] * w[k]
    if b is not None:
        y = y + b
    return y

def rg_lru(x, w_a, b_a, w_x, b_x, lam):
    bsz, s, width = x.shape
    xh = x.reshape(bsz, s, LRU_HEADS, LRU_HEAD_DIM)
    r = jax.nn.sigmoid(jnp.einsum('bshi,hij->bshj', xh, w_a).reshape(bsz, s, width) + b_a)
    i = jax.nn.sigmoid(jnp.einsum('bshi,hij->bshj', xh, w_x).reshape(bsz, s, width) + b_x)
    log_a = -LRU_C * r.astype(jnp.float32) * jax.nn.softplus(-lam.astype(jnp.float32))
    a = jnp.exp(log_a)
    mult = jnp.sqrt(-jnp.expm1(2.0 * log_a))
    reset = (jnp.arange(s) == 0)[None, :, None]
    mult = jnp.where(reset, jnp.ones_like(mult), mult)
    u = mult * (i.astype(jnp.float32) * x.astype(jnp.float32))

    def combine(left, right):
        a_l, b_l = left
        a_r, b_r = right
        return a_l * a_r, a_r * b_l + b_r

    _, h = lax.associative_scan(combine, (a, u), axis=1)
    return h.astype(x.dtype)

def causal_window_mean(x, window):
    s = x.shape[1]
    cs = jnp.cumsum(x.astype(jnp.float32), axis=1)
    lag = jnp.pad(cs, ((0, 0), (window, 0), (0, 0)))[:, :s]
    count = jnp.minimum(jnp.arange(1, s + 1), window).astype(jnp.float32)[None, :, None]
    return ((cs - lag) / count).astype(x.dtype)

def even_mixer(h, w_in, conv_w, conv_b, w_a, b_a, w_x, b_x, lam, sc_conv_w, w_out):
    proj = h @ w_in
    xa, ga, gb_post, gc_pre, v, gb = jnp.split(proj, EVEN_SPLITS, axis=-1)
    ya = rg_lru(causal_dwconv(xa, conv_w, conv_b), w_a, b_a, w_x, b_x, lam)
    yb = gb_post * causal_dwconv(gc_pre * v, sc_conv_w)
    y = jnp.concatenate([ya * jax.nn.silu(ga), yb * jax.nn.silu(gb)], axis=-1)
    return y @ w_out

def odd_mixer(h, w_in, w_grp, b_grp, scale, w_out):
    bsz, s, _ = h.shape
    proj = h @ w_in
    v, g = jnp.split(proj, 2, axis=-1)
    vg = v.reshape(bsz, s, POOL_GROUPS, POOL_GROUP_DIM)
    pooled = jnp.stack([causal_window_mean(vg[:, :, k], POOL_WINDOWS[k])
                        for k in range(POOL_GROUPS)], axis=2)
    mixed = jnp.einsum('bsgc,gcd->bsgd', pooled - vg, w_grp).reshape(bsz, s, POOL_WIDTH) + b_grp
    y = mixed * scale * jax.nn.silu(g)
    return y @ w_out

def setup_inputs(seed: int = 0) -> dict:
    key = jax.random.key(seed)
    ks = jax.random.split(key, 21)
    f32 = jnp.float32
    nrm = lambda k, shape, s: jax.random.normal(k, shape, f32) * s
    d = D_MODEL
    u = jax.random.uniform(ks[12], (N_EVEN, LRU_WIDTH), f32, minval=0.9, maxval=0.999)
    return {
        "x": nrm(ks[0], (BATCH, SEQ, d), 1.0),
        "c": nrm(ks[1], (BATCH, d), 1.0),
        "norm_g": 1.0 + nrm(ks[2], (DEPTH, d), 0.05),
        "mod_w": nrm(ks[3], (DEPTH, d, 3 * d), 0.5 * d ** -0.5),
        "mod_b": nrm(ks[4], (DEPTH, 3 * d), 0.02),
        "hy_w_in": nrm(ks[5], (N_EVEN, d, EVEN_IN), d ** -0.5),
        "hy_conv_w": nrm(ks[6], (N_EVEN, LRU_CONV, LRU_WIDTH), LRU_CONV ** -0.5),
        "hy_conv_b": nrm(ks[7], (N_EVEN, LRU_WIDTH), 0.02),
        "lru_w_a": nrm(ks[8], (N_EVEN, LRU_HEADS, LRU_HEAD_DIM, LRU_HEAD_DIM), LRU_HEAD_DIM ** -0.5),
        "lru_b_a": nrm(ks[9], (N_EVEN, LRU_WIDTH), 0.02),
        "lru_w_x": nrm(ks[10], (N_EVEN, LRU_HEADS, LRU_HEAD_DIM, LRU_HEAD_DIM), LRU_HEAD_DIM ** -0.5),
        "lru_b_x": nrm(ks[11], (N_EVEN, LRU_WIDTH), 0.02),
        "lru_lambda": jnp.log(u) - jnp.log1p(-u),
        "sc_conv_w": nrm(ks[13], (N_EVEN, SC_CONV, SC_WIDTH), SC_CONV ** -0.5),
        "hy_w_out": nrm(ks[14], (N_EVEN, LRU_WIDTH + SC_WIDTH, d), (LRU_WIDTH + SC_WIDTH) ** -0.5),
        "pool_w_in": nrm(ks[15], (N_ODD, d, 2 * POOL_WIDTH), d ** -0.5),
        "pool_w_grp": nrm(ks[16], (N_ODD, POOL_GROUPS, POOL_GROUP_DIM, POOL_GROUP_DIM), POOL_GROUP_DIM ** -0.5),
        "pool_b_grp": nrm(ks[17], (N_ODD, POOL_WIDTH), 0.02),
        "pool_scale": 1.0 + nrm(ks[18], (N_ODD, POOL_WIDTH), 0.1),
        "pool_w_out": nrm(ks[19], (N_ODD, POOL_WIDTH, d), POOL_WIDTH ** -0.5),
        "final_g": 1.0 + nrm(ks[20], (d,), 0.05),
    }

def reference(x, c, norm_g, mod_w, mod_b, hy_w_in, hy_conv_w, hy_conv_b, lru_w_a, lru_b_a,
              lru_w_x, lru_b_x, lru_lambda, sc_conv_w, hy_w_out, pool_w_in, pool_w_grp,
              pool_b_grp, pool_scale, pool_w_out, final_g):
    c_act = jax.nn.silu(c)
    for layer in range(DEPTH):
        mod = c_act @ mod_w[layer] + mod_b[layer]
        shift, scale, gate = jnp.split(mod, 3, axis=-1)
        h = rmsnorm(x, norm_g[layer]) * (1.0 + scale[:, None, :]) + shift[:, None, :]
        if layer % 2 == 0:
            e = layer // 2
            y = even_mixer(h, hy_w_in[e], hy_conv_w[e], hy_conv_b[e], lru_w_a[e], lru_b_a[e],
                           lru_w_x[e], lru_b_x[e], lru_lambda[e], sc_conv_w[e], hy_w_out[e])
        else:
            o = layer // 2
            y = odd_mixer(h, pool_w_in[o], pool_w_grp[o], pool_b_grp[o], pool_scale[o], pool_w_out[o])
        x = x + gate[:, None, :] * y
    return rmsnorm(x, final_g)


_drawn_inputs = setup_inputs


def setup_inputs(seed=0):
    import zlib

    import numpy as np

    out = dict(_drawn_inputs(seed))
    spreads = {}
    factors = {'hy_conv_b': 7.742,
     'lru_b_a': 64.0,
     'lru_b_x': 44.723,
     'pool_b_grp': 8.0,
     'pool_scale': 2.941}
    for name, (base, spread) in spreads.items():
        noise = np.random.default_rng([zlib.crc32(name.encode()), seed]).standard_normal(out[name].shape)
        drawn = base * np.exp(spread * noise) if base else spread * noise
        out[name] = __import__('jax').numpy.asarray(drawn.astype(out[name].dtype))
    for name, factor in factors.items():
        out[name] = (out[name] * factor).astype(out[name].dtype)
    return out
```

```python
from contextlib import ExitStack

import concourse.bass as bass
from concourse import mybir

F32 = mybir.dt.float32
F32R = mybir.dt.float32r
ALU = mybir.AluOpType
ACT = mybir.ActivationFunctionType

P = 128
SLOTS = 4
RAW = 2
HALF = 512
EPS = 1e-6
LRU_C = 8.0
TINY = 2.0 ** -110
WINDOWS = (2, 4, 8, 16)
PAD = max(WINDOWS)

ROWS_A = (("norm_g", 16), ("mod_b", 48), ("conv_w", 32), ("conv_b", 8), ("b_a", 8), ("b_x", 8), ("c", 8))
ROWS_B = (("lam", 8), ("sc_w", 24), ("pool_b", 16), ("pool_scale", 16))
COL = {}
for _name, _n in ROWS_A + ROWS_B:
    COL[_name] = sum(COL[k][1] for k in COL), _n
COL = {k: v[0] for k, v in COL.items()}
NCOL = sum(n for _, n in ROWS_A + ROWS_B)

L0_FIRST = ["xa", "gc", "GM", "v", "r", "i", "ga", "gbp", "gb"]
L0_NEXT = ["xa", "O0", "O1", "gc", "O2", "O3", "v", "O4", "O5", "r", "i", "O6", "O7", "ga", "gbp", "gb"]
L0_UNITS = ["v", "G", "ga", "M0", "gbp", "M1", "WoA", "WoB", "gb", "M2", "xa'", "gc'"]
L0_SPLITS = [u for u in L0_UNITS if u[0] != "M"]
L0_COLS = {"xa": 0, "ga": 1, "gbp": 2, "gc": 3, "v": 4, "gb": 5}

L1_FIRST = ["V0", "V1", "V2", "V3", "G0", "G1", "M0", "M1", "G2", "O0", "O1", "O2", "O3", "G3", "O4", "O5", "O6", "O7",
            "M2", "M3"]
L1_NEXT = ["V0", "Q0", "Q1", "V1", "Q2", "Q3", "V2", "Q4", "Q5", "V3", "Q6", "Q7"] + L1_FIRST[4:]
L1_UNITS = ["V2", "V3", "G0", "G1", "WoA", "WoB", "M01", "G2", "G3", "M23", "WoC", "WoD", "V0'", "V1'"]


class Job:

    def __init__(self, const, turn=0, stride=0):
        self.const, self.turn, self.stride = const, turn, stride
        self.slot = const % SLOTS
        assert stride % SLOTS == 0

    @property
    def full(self):
        return self.turn * self.stride + (self.const + 1)

    @property
    def read(self):
        return self.turn * (self.stride // SLOTS) + (self.const // SLOTS + 1)

    @property
    def free(self):
        return None if self.const < SLOTS and self.stride == 0 else self.turn * (self.stride // SLOTS) + self.const // SLOTS


def build(nc, x, c, norm_g, mod_w, mod_b, hy_w_in, hy_conv_w, hy_conv_b, lru_w_a, lru_b_a, lru_w_x, lru_b_x,
          lru_lambda, sc_conv_w, hy_w_out, pool_w_in, pool_w_grp, pool_b_grp, pool_scale, pool_w_out, final_g, out):
    S, D = x.shape[1:]
    KB = D // P
    SB = S // P
    NH = S // HALF
    HEADS = lru_w_a.shape[1]
    GROUPS = len(WINDOWS)
    GB = pool_w_grp.shape[2] // P
    NMOD = 3 * D
    assert S == D == 1024 and KB == HEADS == 8 and GB == 4 and lru_w_a.shape[2] == P

    J_VEC, J_XT, J_STAT0, J_BC0, J_MOD0 = 0, 1, 1 + KB, 2 + KB, 3 + KB
    J_L0 = J_MOD0 + 1
    J_L0N = J_L0 + len(L0_FIRST)
    J_L0O = J_L0N + (HEADS - 1) * len(L0_NEXT)
    J_MOD1 = J_L0O + KB
    J_STAT1, J_BC1 = J_MOD1 + 1, J_MOD1 + 2
    J_L1 = J_BC1 + 1
    J_L1N = J_L1 + len(L1_FIRST)
    J_L1O = J_L1N + (GROUPS - 1) * len(L1_NEXT)
    J_STAT2 = J_L1O + KB
    J_OUT = J_STAT2 + 1

    def l0_job(name, i, first):
        return Job(J_L0 + L0_FIRST.index(name)) if first else Job(J_L0N + L0_NEXT.index(name), i - 1, len(L0_NEXT))

    def l1_job(name, g, first):
        return Job(J_L1 + L1_FIRST.index(name)) if first else Job(J_L1N + L1_NEXT.index(name), g - 1, len(L1_NEXT))

    def l0_unit(name, i):
        at = 2 + L0_UNITS.index(name)
        return (at % RAW, i * (16 * len(L0_UNITS) // RAW) + 16 * (at // RAW + 1),
                i * len(L0_SPLITS) + (3 + L0_SPLITS.index(name) if name[0] != "M" else 0), i * len(L0_UNITS) + (at + 1))

    U_L1 = 2 + HEADS * len(L0_UNITS)
    N_L1 = 2 + HEADS * len(L0_SPLITS)

    def l1_unit(name, g):
        at = U_L1 + L1_UNITS.index(name)
        return (at % RAW, g * (16 * len(L1_UNITS) // RAW) + 16 * (at // RAW + 1),
                g * len(L1_UNITS) + (N_L1 + 1 + L1_UNITS.index(name)), g * len(L1_UNITS) + (at + 1))

    with ExitStack() as ctx:
        def sb(name, shape, dt=F32, stack=ctx):
            return stack.enter_context(nc.sbuf_tensor(name, shape, dt))

        def sem(name):
            return ctx.enter_context(nc.semaphore(name))

        xT = sb("xT", [P, KB, S])
        h_hi = sb("h_hi", [P, KB, S], F32R)
        h_lo = sb("h_lo", [P, KB, S], F32R)
        w_hi = sb("w_hi", [P, 2, 1024], F32R)
        w_lo = sb("w_lo", [P, 2, 1024], F32R)
        wo_hi = sb("wo_hi", [P, 2, D], F32R)
        wo_lo = sb("wo_lo", [P, 2, D], F32R)
        g_hi = sb("g_hi", [P, 2 * P], F32R)
        g_lo = sb("g_lo", [P, 2 * P], F32R)
        y_hi = sb("y_hi", [P, 2, S], F32R)
        y_lo = sb("y_lo", [P, 2, S], F32R)
        raw = sb("raw", [P, RAW, 1024])
        mod_acc = sb("mod_acc", [P, NMOD])
        vec = sb("vec", [P, NCOL])
        rows_a = sb("rows_a", [P, P])
        rows_b = sb("rows_b", [NCOL - P, P])
        ident = sb("ident", [P, P])
        ones = sb("ones", [P, P])
        modv = sb("modv", [P, 2, 3 * KB])
        gsc = sb("gsc", [P, 2, KB])
        ca = sb("ca", [P, KB])
        sps = sb("sps", [P, 8, HEADS])
        c8 = sb("c8", [P, 2, HEADS])
        cst = sb("cst", [P, 2])
        sd = sb("sd", [P, 3, SB])
        rstd = sb("rstd", [P, 3, SB])
        pos = sb("pos", [P, PAD], mybir.dt.int32)
        icnt = sb("icnt", [P, GROUPS, PAD])
        fix = sb("fix", [P, PAD])

        with ExitStack() as phase:
            st0 = sb("st0", [P, 13, S], F32, phase)
        with ExitStack() as phase:
            xc_hi = sb("xc_hi", [P, S], F32R, phase)
            xc_lo = sb("xc_lo", [P, S], F32R, phase)
            scr = sb("scr", [P, 11, S], F32, phase)
        with ExitStack() as phase:
            d_hi = sb("d_hi", [P, GB, S], F32R, phase)
            d_lo = sb("d_lo", [P, GB, S], F32R, phase)
            sg = sb("sg", [P, 2, S], F32, phase)
            vp = sb("vp", [P, PAD + S], F32, phase)
            win = [sb(f"win{n}", [P, PAD + S], F32, phase) for n in range(2)]
        with ExitStack() as phase:
            ob = sb("ob", [P, SB, D], F32, phase)
        XC, GCS, Z, SC, R, G, TH, A, A2, SGA, SGB = (scr[:, n, :] for n in range(11))
        x_rows, stage, gate_acc = st0[:, 0:SB, :], st0[:, SB:SB + 4, :], st0[:, SB + 4, :]
        psum = ctx.enter_context(nc.psum_tensor("psum", [P, SLOTS, 1024], F32))

        rows_in = sem("rows_in")
        x_in = sem("x_in")
        stage_in = [sem(f"stage_in{n}") for n in range(4)]
        raw_in = [sem(f"raw_in{n}") for n in range(RAW)]
        gate_x_in = sem("gate_x_in")
        fg_in = sem("fg_in")
        out_done = sem("out_done")
        const_step = sem("const_step")
        psum_full = sem("psum_full")
        evacuated = [sem(f"evacuated{n}") for n in range(SLOTS)]
        hi_done = sem("hi_done")
        unit_done = sem("unit_done")
        small = sem("small")
        ca_sig = sem("ca_sig")
        lam_exp = sem("lam_exp")
        stage_used = sem("stage_used")
        sq_ready = sem("sq_ready")
        ssq_added = sem("ssq_added")
        sd_ready = sem("sd_ready")
        diag_ready = sem("diag_ready")
        xn_ready = sem("xn_ready")
        hx_ready = sem("hx_ready")
        hhi_ready = sem("hhi_ready")
        h_ready = sem("h_ready")
        modv_ready = sem("modv_ready")
        conv0 = sem("conv0")
        conv_tap = sem("conv_tap")
        xc_hi_ready = sem("xc_hi_ready")
        xc_ready = sem("xc_ready")
        sc0 = sem("sc0")
        sc_tap = sem("sc_tap")
        gx_done = sem("gx_done")
        th_ready = sem("th_ready")
        a_ready = sem("a_ready")
        a2_ready = sem("a2_ready")
        m2_done = sem("m2_done")
        m_ready = sem("m_ready")
        m_reset = sem("m_reset")
        u_done = sem("u_done")
        scan_done = sem("scan_done")
        sga_ready = sem("sga_ready")
        sgb_ready = sem("sgb_ready")
        y_ready = sem("y_ready")
        yhi_ready = sem("yhi_ready")
        ylo_ready = sem("ylo_ready")
        win_step = sem("win_step")
        d_ready = sem("d_ready")
        dhi_ready = sem("dhi_ready")
        dlo_ready = sem("dlo_ready")
        sg_ready = sem("sg_ready")
        pads = sem("pads")

        def v(name, n=0, count=1):
            return vec[:, bass.ds(COL[name] + n, count)]

        block = ctx.enter_context(nc.Block())

        @block.sync
        def _(sp):
            sp.dma_start(x_rows, x[0].rearrange("(b p) d -> p b d", p=P)).then_inc(x_in, 16)

            def stage_load(slot, k, chunk):
                sp.dma_start(stage[:, slot, :], mod_w[0][bass.ds(k * P, P), chunk * D:(chunk + 1) * D])\
                  .then_inc(stage_in[slot], 16)

            def raw_load(at, src, blocks):
                sp.dma_start(raw[:, at, :].rearrange("p (k n) -> p k n", k=blocks), src).then_inc(raw_in[at], 16)

            hy_in = hy_w_in[0].rearrange("(k p) n -> p k n", p=P)
            pool_in = pool_w_in[0].rearrange("(k p) n -> p k n", p=P)

            for kk in range(2):
                for chunk in range(2):
                    stage_load(2 * kk + chunk, kk, chunk)
            with sp.Fori(1, KB // 2) as t:
                for kk in range(2):
                    for chunk in range(2):
                        sp.wait_ge(stage_used, 4 * (t - 1) + (2 * kk + chunk + 1))
                        stage_load(2 * kk + chunk, 2 * t + kk, chunk)
            raw_load(0, hy_in[:, :, L0_COLS["xa"] * D:L0_COLS["xa"] * D + P], KB)
            raw_load(1, hy_in[:, :, L0_COLS["gc"] * D:L0_COLS["gc"] * D + P], KB)
            with sp.Fori(0, KB // 4) as t:
                for slot in range(4):
                    sp.wait_ge(stage_used, 4 * t + (2 * KB - 4 + slot + 1))
                    stage_load(slot, 4 * t + slot, 2)

            def l0_loads(i, last):
                for name in L0_UNITS:
                    at, _, _, done = l0_unit(name, i)
                    sp.wait_ge(unit_done, done - RAW)
                    if name == "G":
                        sp.dma_start(raw[:, at, 0:P], lru_w_a[0][i]).then_inc(raw_in[at], 16)
                        sp.dma_start(raw[:, at, P:2 * P], lru_w_x[0][i]).then_inc(gate_x_in, 16)
                    elif name[0] == "M":
                        chunk = int(name[1])
                        raw_load(at, mod_w[1][bass.ds(i * P, P), chunk * D:(chunk + 1) * D]
                                 .rearrange("p (k n) -> p k n", k=1), 1)
                    elif name in ("WoA", "WoB"):
                        raw_load(at, hy_w_out[0][bass.ds(i * P + (D if name == "WoB" else 0), P), :]
                                 .rearrange("p (k n) -> p k n", k=1), 1)
                    elif name[-1] != "'":
                        raw_load(at, hy_in[:, :, bass.ds(i * P + L0_COLS[name] * D, P)], KB)
                    elif not last:
                        raw_load(at, hy_in[:, :, bass.ds((i + 1) * P + L0_COLS[name[:-1]] * D, P)], KB)
                    else:
                        n = ("xa'", "gc'").index(name)
                        raw_load(at, pool_in[:, :, n * P:(n + 1) * P], KB)

            with sp.Fori(0, HEADS - 1) as i:
                l0_loads(i, False)
            l0_loads(HEADS - 1, True)

            sp.wait_ge(psum_full, Job(J_MOD1).full)
            sp.dma_start(mod_acc[:, 0:D], final_g.partition_broadcast(P)).then_inc(fg_in, 16)

            def l1_loads(g, last):
                for name in L1_UNITS:
                    if last and name[-1] == "'":
                        continue
                    at, _, _, done = l1_unit(name, g)
                    sp.wait_ge(unit_done, done - RAW)
                    if name[0] == "V":
                        turn = (g + 1) if name[-1] == "'" else g
                        raw_load(at, pool_in[:, :, bass.ds(turn * (GB * P) + int(name[1]) * P, P)], KB)
                    elif name[0] == "G":
                        raw_load(at, pool_in[:, :, bass.ds(g * (GB * P) + (2 * D + int(name[1]) * P), P)], KB)
                    elif name[0] == "M":
                        n = int(name[1]) * P
                        raw_load(at, pool_w_grp[0][g].rearrange("(k p) n -> p k n", p=P)[:, :, n:n + 2 * P], GB)
                    else:
                        raw_load(at, pool_w_out[0][bass.ds(g * (GB * P) + "ABCD".index(name[2]) * P, P), :]
                                 .rearrange("p (k n) -> p k n", k=1), 1)

            with sp.Fori(0, GROUPS - 1) as g:
                l1_loads(g, False)
            l1_loads(GROUPS - 1, True)

            for b in range(SB):
                j = Job(J_OUT + b)
                sp.wait_ge(evacuated[j.slot], j.read)
                sp.dma_start(out[0, b * P:(b + 1) * P, :], ob[:, b, :]).then_inc(out_done, 16)
            sp.wait_ge(out_done, 16 * SB)

        @block.gpsimd
        def _(pool):
            nc.gpsimd.memset(ident[:, :], 0.0).then_inc(const_step, 1)
            nc.gpsimd.memset(ones[:, :], 1.0).then_inc(const_step, 1)
            nc.gpsimd.memset(cst[:, 0:1], EPS).then_inc(const_step, 1)
            nc.gpsimd.memset(cst[:, 1:2], TINY).then_inc(const_step, 1)
            nc.gpsimd.iota(pos[:, :], [[1, PAD]], base=1, channel_multiplier=0).then_inc(const_step, 1)
            pool.wait_ge(const_step, 5)
            nc.gpsimd.affine_select(out=ident[:, :], in_=ident[:, :], compare_op=ALU.not_equal, fill=1.0, base=0,
                                    pattern=[[-1, P]], channel_multiplier=1).then_inc(const_step, 1)

        CONSTS = 6

        @block.scalar
        def _(act):
            at = 0
            for name, src in (("norm_g", norm_g), ("mod_b", mod_b), ("conv_w", hy_conv_w), ("conv_b", hy_conv_b),
                              ("b_a", lru_b_a), ("b_x", lru_b_x), ("c", c), ("lam", lru_lambda), ("sc_w", sc_conv_w),
                              ("pool_b", pool_b_grp), ("pool_scale", pool_scale)):
                n = dict(ROWS_A + ROWS_B)[name]
                dst = rows_a[COL[name]:COL[name] + n, :] if COL[name] < P else rows_b[COL[name] - P:COL[name] - P + n, :]
                letters = "abc"[:len(src.shape) - 1]
                flat = src.rearrange(" ".join(letters) + " (r q) -> (" + " ".join(letters) + " r) q", q=P)
                act.dma_start(dst, flat).then_inc(rows_in, 16)
                at += 1

            def split_hi(dst, unit, n=1024, second=None):
                slot, landed, _, _ = unit
                act.wait_ge(raw_in[slot], landed)
                if second is not None:
                    act.wait_ge(gate_x_in, second)
                nc.scalar.activation(dst, raw[:, slot, 0:n], ACT.Copy).then_inc(hi_done, 1)

            act.wait_ge(small, 2)
            nc.scalar.activation(ca[:, :], v("c", 0, KB), ACT.Sigmoid).then_inc(ca_sig, 1)
            nc.scalar.activation(sps[:, 1, :], sps[:, 0, :], ACT.Exp).then_inc(lam_exp, 1)

            for k in range(KB):
                j = Job(J_XT + k)
                act.wait_ge(psum_full, j.full)
                nc.scalar.activation(xT[:, k, :], psum[:, j.slot, :], ACT.Copy).then_inc(evacuated[j.slot], 1)

            def squares(k, turn, sq):
                if k >= 2:
                    act.wait_ge(ssq_added, turn * KB + k - 1)
                nc.scalar.activation(sq[k % 2], xT[:, k, :], ACT.Square).then_inc(sq_ready, 1)

            def root(turn, job):
                act.wait_ge(psum_full, job.full)
                nc.scalar.activation(sd[:, turn, :], psum[:, job.slot, 0:SB], ACT.Sqrt, scale=1.0 / D,
                                     bias=cst[:, 0:1]).then_inc(sd_ready, 1)

            def modulate(turn, hx):
                for k in range(KB):
                    n = turn * KB + k
                    act.wait_ge(xn_ready, n + 1)
                    nc.scalar.activation(hx[k % 4], hx[k % 4], ACT.Identity, scale=gsc[:, turn, k:k + 1],
                                         bias=modv[:, turn, k:k + 1]).then_inc(hx_ready, 1)
                    act.wait_ge(hx_ready, n + 1)
                    nc.scalar.activation(h_hi[:, k, :], hx[k % 4], ACT.Copy).then_inc(hhi_ready, 1)

            for k in range(KB):
                act.wait_ge(evacuated[Job(J_XT + k).slot], Job(J_XT + k).read)
                if k == 0:
                    act.wait_ge(psum_full, J_XT + KB)
                squares(k, 0, (x_rows[:, 0, :], x_rows[:, 1, :]))
            root(0, Job(J_STAT0))
            act.wait_ge(modv_ready, 1)
            split_hi(w_hi[:, 0, :], (0, 16, None, None))
            split_hi(w_hi[:, 1, :], (1, 16, None, None))
            modulate(0, [x_rows[:, 4 + n, :] for n in range(4)])

            def l0(i, first):
                def job(name):
                    return l0_job(name, i, first)

                act.wait_ge(psum_full, job("xa").full)
                split_hi(w_hi[:, 0, :], l0_unit("v", i))
                if not first:
                    act.wait_ge(gx_done, i)
                nc.scalar.activation(XC, psum[:, job("xa").slot, :], ACT.Identity, scale=v("conv_w", 3 * HEADS + i),
                                     bias=v("conv_b", i)).then_inc(conv0, 1)
                split_hi(g_hi[:, :], l0_unit("G", i), 2 * P, 16 * (i + 1))
                act.wait_ge(evacuated[job("xa").slot], job("xa").read)
                nc.scalar.activation(xc_hi[:, :], XC, ACT.Copy).then_inc(xc_hi_ready, 1)
                act.wait_ge(psum_full, job("gc").full)
                split_hi(w_hi[:, 1, :], l0_unit("ga", i))
                nc.scalar.activation(GCS, psum[:, job("gc").slot, :], ACT.Copy).then_inc(evacuated[job("gc").slot], 1)
                act.wait_ge(psum_full, job("v").full)
                split_hi(w_hi[:, 0, :], l0_unit("gbp", i))
                act.wait_ge(evacuated[job("v").slot], job("v").read)
                if not first:
                    act.wait_ge(y_ready, 2 * i)
                nc.scalar.activation(SC, Z, ACT.Copy, scale=v("sc_w", 2 * HEADS + i)).then_inc(sc0, 1)
                act.wait_ge(psum_full, job("r").full)
                nc.scalar.activation(R, psum[:, job("r").slot, :], ACT.Sigmoid, bias=v("b_a", i))\
                  .then_inc(evacuated[job("r").slot], 1)
                act.wait_ge(psum_full, job("i").full)
                nc.scalar.activation(G, psum[:, job("i").slot, :], ACT.Sigmoid, bias=v("b_x", i))\
                  .then_inc(evacuated[job("i").slot], 1)
                act.wait_ge(evacuated[job("r").slot], job("r").read)
                nc.scalar.activation(TH, R, ACT.Tanh, scale=c8[:, 0, bass.ds(i, 1)]).then_inc(th_ready, 1)
                nc.scalar.activation(A, R, ACT.Exp, scale=c8[:, 1, bass.ds(i, 1)]).then_inc(a_ready, 1)
                act.wait_ge(a_ready, i + 1)
                nc.scalar.activation(A2, A, ACT.Square).then_inc(a2_ready, 1)
                act.wait_ge(m2_done, i + 1)
                nc.scalar.activation(A2, TH, ACT.Sqrt, bias=cst[:, 1:2]).then_inc(m_ready, 1)
                if not first:
                    act.wait_ge(psum_full, job("O7").full)
                split_hi(wo_hi[:, 0, :], l0_unit("WoA", i))
                split_hi(wo_hi[:, 1, :], l0_unit("WoB", i))
                act.wait_ge(psum_full, job("ga").full)
                split_hi(w_hi[:, 1, :], l0_unit("gb", i))
                nc.scalar.activation(SGA, psum[:, job("ga").slot, :], ACT.Sigmoid).then_inc(sga_ready, 1)
                act.wait_ge(psum_full, job("gbp").full)
                split_hi(w_hi[:, 0, :], l0_unit("xa'", i))
                act.wait_ge(y_ready, 2 * i + 1)
                nc.scalar.activation(y_hi[:, 0, :], SGA, ACT.Copy).then_inc(yhi_ready, 1)
                act.wait_ge(psum_full, job("gb").full)
                split_hi(w_hi[:, 1, :], l0_unit("gc'", i))
                nc.scalar.activation(SGB, psum[:, job("gb").slot, :], ACT.Sigmoid).then_inc(sgb_ready, 1)
                act.wait_ge(y_ready, 2 * i + 2)
                nc.scalar.activation(y_hi[:, 1, :], SGB, ACT.Copy).then_inc(yhi_ready, 1)

            l0(0, True)
            with act.Fori(1, HEADS) as i:
                l0(i, False)

            for k in range(KB):
                act.wait_ge(evacuated[Job(J_L0O + k).slot], Job(J_L0O + k).read)
                squares(k, 1, (scr[:, 0, :], scr[:, 1, :]))
            root(1, Job(J_STAT1))
            act.wait_ge(modv_ready, 2)
            modulate(1, [scr[:, 4 + n, :] for n in range(4)])

            def l1(g, first, last):
                def job(name):
                    return l1_job(name, g, first)

                def unit(name):
                    return l1_unit(name, g)

                def pair_y(n):
                    for m in range(2):
                        j = job(f"M{n + m}")
                        act.wait_ge(evacuated[j.slot], j.read)
                        nc.scalar.activation(y_hi[:, m, :], sg[:, m, :], ACT.Copy).then_inc(yhi_ready, 1)

                def gates(n):
                    j = job(f"G{n}")
                    act.wait_ge(ylo_ready, GB * g + (2 * HEADS + n - 1))
                    nc.scalar.activation(sg[:, n % 2, :], psum[:, j.slot, :], ACT.Sigmoid).then_inc(sg_ready, 1)

                for n in range(GB):
                    j = job(f"V{n}")
                    act.wait_ge(psum_full, j.full)
                    split_hi(w_hi[:, n % 2, :], unit(("V2", "V3", "G0", "G1")[n]))
                    if n or not first:
                        act.wait_ge(dlo_ready, GB * g + n)
                    nc.scalar.activation(vp[:, PAD:], psum[:, j.slot, :], ACT.Copy).then_inc(evacuated[j.slot], 1)
                    act.wait_ge(d_ready, GB * g + (n + 1))
                    nc.scalar.activation(d_hi[:, n, :], vp[:, PAD:], ACT.Copy).then_inc(dhi_ready, 1)
                if not first:
                    act.wait_ge(psum_full, job("Q7").full)
                split_hi(wo_hi[:, 0, :], unit("WoA"))
                split_hi(wo_hi[:, 1, :], unit("WoB"))
                act.wait_ge(psum_full, job("G0").full)
                split_hi(w_hi[:, 0, :], unit("M01"))
                gates(0)
                act.wait_ge(psum_full, job("G1").full)
                split_hi(w_hi[:, 1, :], unit("G2"))
                gates(1)
                act.wait_ge(psum_full, job("M1").full)
                split_hi(w_hi[:, 0, :], unit("G3"))
                pair_y(0)
                act.wait_ge(psum_full, job("G2").full)
                split_hi(w_hi[:, 1, :], unit("M23"))
                gates(2)
                act.wait_ge(psum_full, job("G3").full)
                gates(3)
                act.wait_ge(psum_full, job("O7").full)
                split_hi(wo_hi[:, 0, :], unit("WoC"))
                split_hi(wo_hi[:, 1, :], unit("WoD"))
                if not last:
                    split_hi(w_hi[:, 0, :], unit("V0'"))
                act.wait_ge(psum_full, job("M3").full)
                if not last:
                    split_hi(w_hi[:, 1, :], unit("V1'"))
                pair_y(2)

            l1(0, True, False)
            with act.Fori(1, GROUPS - 1) as g:
                l1(g, False, False)
            l1(GROUPS - 1, False, True)

            for k in range(KB):
                act.wait_ge(evacuated[Job(J_L1O + k).slot], Job(J_L1O + k).read)
                if k == 0:
                    act.wait_ge(ylo_ready, 2 * HEADS + GB * GROUPS)
                squares(k, 2, (sg[:, 0, :], sg[:, 1, :]))
            root(2, Job(J_STAT2))

        @block.vector
        def _(dve):
            smalls = [0]

            def step(ins):
                smalls[0] += 1
                ins.then_inc(small, 1)
                dve.wait_ge(small, smalls[0])

            def split_lo(dst, hi, unit, n=1024):
                slot, _, done, _ = unit
                dve.wait_ge(hi_done, done)
                nc.vector.tensor_tensor(dst, raw[:, slot, 0:n], hi.bitcast(F32), ALU.subtract).then_inc(unit_done, 1)

            j = Job(J_VEC)
            dve.wait_ge(psum_full, j.full)
            nc.vector.tensor_copy(vec[:, :], psum[:, j.slot, 0:NCOL]).then_inc(evacuated[j.slot], 1)
            dve.wait_ge(evacuated[j.slot], j.read)
            step(nc.vector.tensor_scalar(sps[:, 0, :], v("lam", 0, HEADS), -1.0, None, ALU.mult))
            step(nc.vector.tensor_tensor(sps[:, 0, :], sps[:, 0, :], v("lam", 0, HEADS), ALU.min))
            dve.wait_ge(ca_sig, 1)
            step(nc.vector.tensor_tensor(ca[:, :], ca[:, :], v("c", 0, KB), ALU.mult))
            step(nc.vector.memset(mod_acc[:, :], 0.0))
            step(nc.vector.memset(gate_acc, 0.0))

            def add_unit(dst, src, k, signal):
                nc.vector.scalar_tensor_tensor(out=dst, in0=src, scalar=ca[:, bass.ds(k, 1)], in1=dst, op0=ALU.mult,
                                               op1=ALU.add).then_inc(signal, 1)

            def add_stage(t, first):
                for kk in range(2):
                    for chunk in range(2):
                        slot = 2 * kk + chunk
                        dve.wait_ge(stage_in[slot], 16 * (t + 1))
                        if not first or kk:
                            dve.wait_ge(stage_used, 4 * t + (slot - 1))
                        add_unit(mod_acc[:, chunk * D:(chunk + 1) * D], stage[:, slot, :], 2 * t + kk, stage_used)


            def modulation(layer, blocks, job):
                lo, hi = blocks
                dve.wait_ge(psum_full, job.full)
                at = COL["mod_b"] + layer * 3 * KB
                nc.vector.tensor_tensor(modv[:, layer, lo:hi], psum[:, job.slot, 0:hi - lo],
                                        vec[:, at + lo:at + hi], ALU.add).then_inc(evacuated[job.slot], 1)

            def scale_norm(layer, job):
                dve.wait_ge(evacuated[job.slot], job.read)
                nc.vector.scalar_tensor_tensor(out=gsc[:, layer, :], in0=modv[:, layer, KB:2 * KB], scalar=1.0,
                                               in1=vec[:, COL["norm_g"] + layer * KB:COL["norm_g"] + (layer + 1) * KB],
                                               op0=ALU.add, op1=ALU.mult).then_inc(modv_ready, 1)

            def sum_squares(k, turn, sq, ssq):
                dve.wait_ge(sq_ready, turn * KB + k + 1)
                if k == 0:
                    ins = nc.vector.tensor_copy(ssq, sq[0])
                else:
                    dve.wait_ge(ssq_added, turn * KB + k)
                    ins = nc.vector.tensor_tensor(ssq, ssq, sq[k % 2], ALU.add)
                ins.then_inc(ssq_added, 1)

            def inverse(turn, job):
                dve.wait_ge(sd_ready, turn + 1)
                nc.vector.reciprocal(rstd[:, turn, :], sd[:, turn, :]).then_inc(evacuated[job.slot], 1)
                dve.wait_ge(evacuated[job.slot], job.read)

            def diagonals(turn, diag):
                for b in range(SB):
                    ins = nc.vector.tensor_scalar(diag[:, b * P:(b + 1) * P], ident[:, :], rstd[:, turn, b:b + 1], None,
                                                  ALU.mult)
                ins.then_inc(diag_ready, 1)

            def normalize(turn, job, hx):
                dve.wait_ge(psum_full, job.full)
                for k in range(KB + 2):
                    n = turn * KB + k
                    if k < KB:
                        if k >= 4:
                            dve.wait_ge(h_ready, turn * (KB - 1) + k - 3)
                        nc.vector.tensor_tensor(hx[k % 4], xT[:, k, :], psum[:, job.slot, :], ALU.mult)\
                          .then_inc(xn_ready, 1)
                    if k >= 2:
                        dve.wait_ge(hhi_ready, n - 1)
                        nc.vector.tensor_tensor(h_lo[:, k - 2, :], hx[(k - 2) % 4], h_hi[:, k - 2, :].bitcast(F32),
                                                ALU.subtract)\
                          .then_inc(h_ready if k < KB + 1 else evacuated[job.slot], 1)

            E_, S_, S2, T_, M_ = (sps[:, n, :] for n in (1, 2, 3, 4, 5))
            dve.wait_ge(lam_exp, 1)
            step(nc.vector.tensor_scalar(T_, E_, 2.0, None, ALU.add))
            step(nc.vector.reciprocal(S_, T_))
            step(nc.vector.tensor_tensor(S_, S_, E_, ALU.mult))
            step(nc.vector.tensor_tensor(S2, S_, S_, ALU.mult))
            TERMS = 9
            step(nc.vector.tensor_scalar(T_, S2, 1.0 / (2 * TERMS + 1), 1.0 / (2 * TERMS - 1), ALU.mult, ALU.add))
            for n in range(TERMS - 2, -1, -1):
                step(nc.vector.tensor_tensor(T_, T_, S2, ALU.mult))
                step(nc.vector.tensor_scalar(T_, T_, 1.0 / (2 * n + 1), None, ALU.add))
            step(nc.vector.tensor_tensor(T_, T_, S_, ALU.mult))
            step(nc.vector.tensor_scalar(M_, v("lam", 0, HEADS), -1.0, 0.0, ALU.mult, ALU.max))
            step(nc.vector.scalar_tensor_tensor(out=M_, in0=T_, scalar=2.0, in1=M_, op0=ALU.mult, op1=ALU.add))
            step(nc.vector.tensor_scalar(c8[:, 0, :], M_, LRU_C, None, ALU.mult))
            step(nc.vector.tensor_scalar(c8[:, 1, :], M_, -LRU_C, None, ALU.mult))
            dve.wait_ge(const_step, CONSTS)
            step(nc.vector.tensor_copy(fix[:, :], pos[:, :]))
            for n, window in enumerate(WINDOWS):
                step(nc.vector.tensor_scalar(icnt[:, n, :], fix[:, :], float(window), None, ALU.min))
                step(nc.vector.reciprocal(icnt[:, n, :], icnt[:, n, :]))
            for k in range(KB):
                sum_squares(k, 0, (x_rows[:, 0, :], x_rows[:, 1, :]), x_rows[:, 2, :])
            inverse(0, Job(J_STAT0))
            diagonals(0, x_rows[:, 3, :])
            add_stage(0, True)
            with dve.Fori(1, KB // 2) as t:
                add_stage(t, False)
            modulation(0, (0, 2 * KB), Job(J_MOD0))
            scale_norm(0, Job(J_MOD0))
            split_lo(w_lo[:, 0, :], w_hi[:, 0, :], (0, None, 1, None))
            split_lo(w_lo[:, 1, :], w_hi[:, 1, :], (1, None, 2, None))
            normalize(0, Job(J_BC0), [x_rows[:, 4 + n, :] for n in range(4)])
            step(nc.vector.memset(mod_acc[:, :], 0.0))

            with dve.Fori(0, KB // 4) as t:
                for slot in range(4):
                    dve.wait_ge(stage_in[slot], 16 * t + 16 * (KB // 2 + 1))
                    dve.wait_ge(stage_used, 4 * t + (2 * KB + slot))
                    add_unit(gate_acc, stage[:, slot, :], 4 * t + slot, stage_used)

            def residual(k, layer, job):
                dve.wait_ge(psum_full, job.full)
                nc.vector.scalar_tensor_tensor(out=xT[:, k, :], in0=psum[:, job.slot, :],
                                               scalar=modv[:, layer, 2 * KB + k:2 * KB + k + 1], in1=xT[:, k, :],
                                               op0=ALU.mult, op1=ALU.add).then_inc(evacuated[job.slot], 1)

            def add_mod(i, chunk):
                slot, landed, _, done = l0_unit(f"M{chunk}", i)
                dve.wait_ge(raw_in[slot], landed)
                dve.wait_ge(unit_done, done - 1)
                add_unit(mod_acc[:, chunk * D:(chunk + 1) * D], raw[:, slot, :], i, unit_done)

            def l0(i, first):
                def job(name):
                    return l0_job(name, i, first)

                def outs(*blocks):
                    if not first:
                        for k in blocks:
                            residual(k, 0, job(f"O{k}"))

                split_lo(w_lo[:, 0, :], w_hi[:, 0, :], l0_unit("v", i))
                xa = job("xa")
                dve.wait_ge(conv0, i + 1)
                for n, back in enumerate((1, 2, 3)):
                    if n:
                        dve.wait_ge(conv_tap, 2 * i + n)
                    nc.vector.scalar_tensor_tensor(out=XC[:, back:], in0=psum[:, xa.slot, 0:S - back],
                                                   scalar=v("conv_w", (3 - back) * HEADS + i), in1=XC[:, back:],
                                                   op0=ALU.mult, op1=ALU.add)\
                      .then_inc(conv_tap if n < 2 else evacuated[xa.slot], 1)
                split_lo(g_lo[:, :], g_hi[:, :], l0_unit("G", i), 2 * P)
                outs(0, 1)
                dve.wait_ge(xc_hi_ready, i + 1)
                nc.vector.tensor_tensor(xc_lo[:, :], XC, xc_hi[:, :].bitcast(F32), ALU.subtract).then_inc(xc_ready, 1)
                split_lo(w_lo[:, 1, :], w_hi[:, 1, :], l0_unit("ga", i))
                if first:
                    modulation(0, (2 * KB, 3 * KB), job("GM"))
                    dve.wait_ge(evacuated[job("GM").slot], job("GM").read)
                add_mod(i, 0)
                outs(2, 3)
                split_lo(w_lo[:, 0, :], w_hi[:, 0, :], l0_unit("gbp", i))
                gc, vj = job("gc"), job("v")
                dve.wait_ge(evacuated[gc.slot], gc.read)
                dve.wait_ge(psum_full, vj.full)
                nc.vector.tensor_tensor(Z, psum[:, vj.slot, :], GCS, ALU.mult).then_inc(evacuated[vj.slot], 1)
                add_mod(i, 1)
                dve.wait_ge(sc0, i + 1)
                for n, back in enumerate((1, 2)):
                    if n:
                        dve.wait_ge(sc_tap, 2 * i + 1)
                    nc.vector.scalar_tensor_tensor(out=SC[:, back:], in0=Z[:, 0:S - back],
                                                   scalar=v("sc_w", (2 - back) * HEADS + i), in1=SC[:, back:],
                                                   op0=ALU.mult, op1=ALU.add).then_inc(sc_tap, 1)
                outs(4, 5)
                ij = job("i")
                dve.wait_ge(evacuated[ij.slot], ij.read)
                nc.vector.tensor_tensor(G, G, XC, ALU.mult).then_inc(gx_done, 1)
                dve.wait_ge(th_ready, i + 1)
                dve.wait_ge(a2_ready, i + 1)
                nc.vector.scalar_tensor_tensor(out=TH, in0=A2, scalar=1.0, in1=TH, op0=ALU.add, op1=ALU.mult)\
                  .then_inc(m2_done, 1)
                outs(6, 7)
                dve.wait_ge(m_ready, i + 1)
                nc.vector.memset(A2[:, 0:1], 1.0).then_inc(m_reset, 1)
                dve.wait_ge(m_reset, i + 1)
                dve.wait_ge(gx_done, i + 1)
                nc.vector.tensor_tensor(G, G, A2, ALU.mult).then_inc(u_done, 1)
                dve.wait_ge(u_done, i + 1)
                nc.vector.tensor_tensor_scan(R, A, G, 0.0, ALU.mult, ALU.add).then_inc(scan_done, 1)
                split_lo(wo_lo[:, 0, :], wo_hi[:, 0, :], l0_unit("WoA", i))
                split_lo(wo_lo[:, 1, :], wo_hi[:, 1, :], l0_unit("WoB", i))
                split_lo(w_lo[:, 1, :], w_hi[:, 1, :], l0_unit("gb", i))
                ga = job("ga")
                dve.wait_ge(sga_ready, i + 1)
                nc.vector.tensor_tensor(SGA, psum[:, ga.slot, :], SGA, ALU.mult).then_inc(evacuated[ga.slot], 1)
                dve.wait_ge(evacuated[ga.slot], ga.read)
                dve.wait_ge(scan_done, i + 1)
                nc.vector.tensor_tensor(SGA, SGA, R, ALU.mult).then_inc(y_ready, 1)
                add_mod(i, 2)
                split_lo(w_lo[:, 0, :], w_hi[:, 0, :], l0_unit("xa'", i))
                gbp = job("gbp")
                dve.wait_ge(psum_full, gbp.full)
                dve.wait_ge(sc_tap, 2 * i + 2)
                nc.vector.tensor_tensor(SC, psum[:, gbp.slot, :], SC, ALU.mult).then_inc(evacuated[gbp.slot], 1)
                dve.wait_ge(yhi_ready, 2 * i + 1)
                nc.vector.tensor_tensor(y_lo[:, 0, :], SGA, y_hi[:, 0, :].bitcast(F32), ALU.subtract)\
                  .then_inc(ylo_ready, 1)
                split_lo(w_lo[:, 1, :], w_hi[:, 1, :], l0_unit("gc'", i))
                gb = job("gb")
                dve.wait_ge(sgb_ready, i + 1)
                nc.vector.tensor_tensor(SGB, psum[:, gb.slot, :], SGB, ALU.mult).then_inc(evacuated[gb.slot], 1)
                dve.wait_ge(evacuated[gb.slot], gb.read)
                dve.wait_ge(evacuated[gbp.slot], gbp.read)
                nc.vector.tensor_tensor(SGB, SGB, SC, ALU.mult).then_inc(y_ready, 1)
                dve.wait_ge(yhi_ready, 2 * i + 2)
                nc.vector.tensor_tensor(y_lo[:, 1, :], SGB, y_hi[:, 1, :].bitcast(F32), ALU.subtract)\
                  .then_inc(ylo_ready, 1)

            l0(0, True)
            with dve.Fori(1, HEADS) as i:
                l0(i, False)

            sq, ssq = (scr[:, 0, :], scr[:, 1, :]), scr[:, 2, :]
            for k in range(KB + 1):
                if k < KB:
                    residual(k, 0, Job(J_L0O + k))
                if k:
                    sum_squares(k - 1, 1, sq, ssq)
            modulation(1, (0, 3 * KB), Job(J_MOD1))
            scale_norm(1, Job(J_MOD1))
            inverse(1, Job(J_STAT1))
            diagonals(1, scr[:, 3, :])
            normalize(1, Job(J_BC1), [scr[:, 4 + n, :] for n in range(4)])

            for buf in (vp, *win):
                nc.vector.memset(buf[:, 0:PAD], 0.0).then_inc(pads, 1)
            dve.wait_ge(pads, 3)

            sums = [0]

            def l1(g):
                first = g == 0

                def job(name):
                    return l1_job(name, g, first)

                def unit(name):
                    return l1_unit(name, g)

                def window_step(ins):
                    sums[0] += 1
                    ins.then_inc(win_step, 1)
                    dve.wait_ge(win_step, sums[0])

                def queued(*blocks):
                    if not first:
                        for k in blocks:
                            residual(k, 1, job(f"Q{k}"))

                def outs(*blocks):
                    for k in blocks:
                        residual(k, 1, job(f"O{k}"))

                def pool_block(n):
                    vj = job(f"V{n}")
                    dve.wait_ge(evacuated[vj.slot], vj.read)
                    src, width, turn = vp, 1, 0
                    while width < WINDOWS[g]:
                        dst = win[turn % 2]
                        window_step(nc.vector.tensor_tensor(dst[:, width:], src[:, width:], src[:, 0:PAD + S - width],
                                                            ALU.add))
                        src, width, turn = dst, 2 * width, turn + 1
                    window_step(nc.vector.tensor_tensor(fix[:, :], src[:, PAD:2 * PAD], icnt[:, g, :], ALU.mult))
                    window_step(nc.vector.tensor_tensor(vp[:, PAD:2 * PAD], fix[:, :], vp[:, PAD:2 * PAD], ALU.subtract))
                    nc.vector.scalar_tensor_tensor(out=vp[:, 2 * PAD:], in0=src[:, 2 * PAD:], scalar=1.0 / WINDOWS[g],
                                                   in1=vp[:, 2 * PAD:], op0=ALU.mult, op1=ALU.subtract)\
                      .then_inc(d_ready, 1)

                def pool_lo(n):
                    dve.wait_ge(dhi_ready, GB * g + n + 1)
                    nc.vector.tensor_tensor(d_lo[:, n, :], vp[:, PAD:], d_hi[:, n, :].bitcast(F32), ALU.subtract)\
                      .then_inc(dlo_ready, 1)

                def gates(n):
                    j = job(f"G{n}")
                    dve.wait_ge(sg_ready, GB * g + n + 1)
                    nc.vector.scalar_tensor_tensor(out=sg[:, n % 2, :], in0=psum[:, j.slot, :],
                                                   scalar=v("pool_scale", GB * g + n), in1=sg[:, n % 2, :],
                                                   op0=ALU.mult, op1=ALU.mult).then_inc(evacuated[j.slot], 1)

                def mixed(n):
                    j, gj = job(f"M{n}"), job(f"G{n}")
                    dve.wait_ge(evacuated[gj.slot], gj.read)
                    dve.wait_ge(psum_full, j.full)
                    nc.vector.scalar_tensor_tensor(out=sg[:, n % 2, :], in0=psum[:, j.slot, :],
                                                   scalar=v("pool_b", GB * g + n), in1=sg[:, n % 2, :],
                                                   op0=ALU.add, op1=ALU.mult).then_inc(evacuated[j.slot], 1)

                def mixed_lo(n):
                    dve.wait_ge(yhi_ready, 2 * HEADS + GB * g + n + 1)
                    nc.vector.tensor_tensor(y_lo[:, n % 2, :], sg[:, n % 2, :], y_hi[:, n % 2, :].bitcast(F32),
                                            ALU.subtract).then_inc(ylo_ready, 1)

                for n in range(GB):
                    split_lo(w_lo[:, n % 2, :], w_hi[:, n % 2, :], unit(("V2", "V3", "G0", "G1")[n]))
                    pool_block(n)
                    queued(2 * n, 2 * n + 1)
                    pool_lo(n)
                split_lo(wo_lo[:, 0, :], wo_hi[:, 0, :], unit("WoA"))
                split_lo(wo_lo[:, 1, :], wo_hi[:, 1, :], unit("WoB"))
                split_lo(w_lo[:, 0, :], w_hi[:, 0, :], unit("M01"))
                gates(0)
                split_lo(w_lo[:, 1, :], w_hi[:, 1, :], unit("G2"))
                gates(1)
                mixed(0)
                split_lo(w_lo[:, 0, :], w_hi[:, 0, :], unit("G3"))
                mixed(1)
                mixed_lo(0)
                mixed_lo(1)
                split_lo(w_lo[:, 1, :], w_hi[:, 1, :], unit("M23"))
                gates(2)
                outs(0, 1, 2, 3)
                gates(3)
                outs(4, 5, 6, 7)
                split_lo(wo_lo[:, 0, :], wo_hi[:, 0, :], unit("WoC"))
                split_lo(wo_lo[:, 1, :], wo_hi[:, 1, :], unit("WoD"))
                if g < GROUPS - 1:
                    split_lo(w_lo[:, 0, :], w_hi[:, 0, :], unit("V0'"))
                mixed(2)
                mixed(3)
                if g < GROUPS - 1:
                    split_lo(w_lo[:, 1, :], w_hi[:, 1, :], unit("V1'"))
                mixed_lo(2)
                mixed_lo(3)

            for g in range(GROUPS):
                l1(g)

            sq, ssq = (sg[:, 0, :], sg[:, 1, :]), vp[:, PAD:]
            for k in range(KB + 1):
                if k < KB:
                    residual(k, 1, Job(J_L1O + k))
                if k:
                    sum_squares(k - 1, 2, sq, ssq)
            inverse(2, Job(J_STAT2))
            dve.wait_ge(fg_in, 16)
            for b in range(SB):
                j = Job(J_OUT + b)
                dve.wait_ge(psum_full, j.full)
                nc.vector.scalar_tensor_tensor(out=ob[:, b, :], in0=psum[:, j.slot, :], scalar=rstd[:, 2, b:b + 1],
                                               in1=mod_acc[:, 0:D], op0=ALU.mult, op1=ALU.mult)\
                  .then_inc(evacuated[j.slot], 1)

        @block.tensor
        def _(pe):
            def take(job):
                if job.const >= SLOTS or not isinstance(job.turn, int):
                    pe.wait_ge(evacuated[job.slot], job.free)

            def product(job, blocks):
                take(job)
                dst = psum[:, job.slot, :]
                for n, (whi, wlo, xhi, xlo) in enumerate(blocks):
                    first, last = n == 0, n == len(blocks) - 1
                    for hh in range(NH):
                        cols = slice(hh * HALF, (hh + 1) * HALF)
                        nc.tensor.matmul(dst[:, cols], whi, xhi[:, cols], start=first, stop=False)
                        nc.tensor.matmul(dst[:, cols], whi, xlo[:, cols], start=False, stop=False)
                    for hh in range(NH):
                        cols = slice(hh * HALF, (hh + 1) * HALF)
                        ins = nc.tensor.matmul(dst[:, cols], wlo, xhi[:, cols], start=False, stop=last)
                ins.then_inc(psum_full, 1)

            def project(job, slot):
                product(job, [(w_hi[:, slot, k * P:(k + 1) * P], w_lo[:, slot, k * P:(k + 1) * P], h_hi[:, k, :],
                               h_lo[:, k, :]) for k in range(KB)])

            def out_project(job, k):
                product(job, [(wo_hi[:, m, k * P:(k + 1) * P], wo_lo[:, m, k * P:(k + 1) * P], y_hi[:, m, :],
                               y_lo[:, m, :]) for m in range(2)])

            def column_sums(job, acc, blocks):
                take(job)
                for n in range(blocks):
                    ins = nc.tensor.matmul(psum[:, job.slot, n:n + 1], acc[:, n * P:(n + 1) * P], ones[:, 0:1],
                                           start=True, stop=True)
                ins.then_inc(psum_full, 1)

            def broadcast(job, turn, diag):
                take(job)
                pe.wait_ge(diag_ready, turn + 1)
                for hh in range(NH):
                    cols = slice(hh * HALF, (hh + 1) * HALF)
                    ins = nc.tensor.matmul(psum[:, job.slot, cols], ones[:, :], diag[:, cols], start=True, stop=True)
                ins.then_inc(psum_full, 1)

            pe.wait_ge(const_step, CONSTS)
            pe.wait_ge(rows_in, 16 * (len(ROWS_A) + len(ROWS_B)))
            nc.tensor.transpose(psum[:, J_VEC, 0:P], rows_a[:, :], ident[:, :])
            nc.tensor.transpose(psum[:, J_VEC, P:NCOL], rows_b[:, :], ident[0:NCOL - P, 0:NCOL - P])\
              .then_inc(psum_full, 1)
            pe.wait_ge(x_in, 16)
            for k in range(KB):
                j = Job(J_XT + k)
                take(j)
                for b in range(SB):
                    ins = nc.tensor.transpose(psum[:, j.slot, b * P:(b + 1) * P], x_rows[:, b, k * P:(k + 1) * P],
                                              ident[:, :])
                ins.then_inc(psum_full, 1)

            pe.wait_ge(ssq_added, KB)
            column_sums(Job(J_STAT0), x_rows[:, 2, :], SB)
            broadcast(Job(J_BC0), 0, x_rows[:, 3, :])
            pe.wait_ge(stage_used, 2 * KB)
            column_sums(Job(J_MOD0), mod_acc, 2 * KB)

            def l0(i, first):
                for name in (L0_FIRST if first else L0_NEXT):
                    j = l0_job(name, i, first)
                    if name[0] == "O":
                        k = int(name[1])
                        if k == 0:
                            pe.wait_ge(ylo_ready, 2 * i)
                            pe.wait_ge(unit_done, l0_unit("WoB", i - 1)[3])
                        out_project(j, k)
                    elif name == "GM":
                        pe.wait_ge(stage_used, 3 * KB)
                        column_sums(j, gate_acc, KB)
                    elif name in ("r", "i"):
                        if name == "r":
                            pe.wait_ge(xc_ready, i + 1)
                            pe.wait_ge(unit_done, l0_unit("G", i)[3])
                        at = slice(0, P) if name == "r" else slice(P, 2 * P)
                        product(j, [(g_hi[:, at], g_lo[:, at], xc_hi[:, :], xc_lo[:, :])])
                    else:
                        slot = ("xa", "gc", "v", "ga", "gbp", "gb").index(name) % 2
                        if name not in ("xa", "gc"):
                            pe.wait_ge(unit_done, l0_unit(name, i)[3])
                        elif first:
                            pe.wait_ge(unit_done, 1 + slot)
                            if name == "xa":
                                pe.wait_ge(evacuated[Job(J_BC0).slot], Job(J_BC0).read)
                        else:
                            pe.wait_ge(unit_done, l0_unit(name + "'", i - 1)[3])
                        project(j, slot)

            l0(0, True)
            with pe.Fori(1, HEADS) as i:
                l0(i, False)
            pe.wait_ge(ylo_ready, 2 * HEADS)
            pe.wait_ge(unit_done, l0_unit("WoB", HEADS - 1)[3])
            for k in range(KB):
                out_project(Job(J_L0O + k), k)
            pe.wait_ge(unit_done, l0_unit("M2", HEADS - 1)[3])
            column_sums(Job(J_MOD1), mod_acc, 3 * KB)
            pe.wait_ge(ssq_added, 2 * KB)
            column_sums(Job(J_STAT1), scr[:, 2, :], SB)
            broadcast(Job(J_BC1), 1, scr[:, 3, :])

            def l1(g, first):
                for name in (L1_FIRST if first else L1_NEXT):
                    j = l1_job(name, g, first)
                    n = int(name[1])
                    if name[0] in "QO":
                        if n == 0 and name[0] == "Q":
                            pe.wait_ge(ylo_ready, GB * g + 2 * HEADS)
                            pe.wait_ge(unit_done, l1_unit("WoD", g - 1)[3])
                        elif n == 0:
                            pe.wait_ge(ylo_ready, GB * g + (2 * HEADS + 2))
                            pe.wait_ge(unit_done, l1_unit("WoB", g)[3])
                        out_project(j, n)
                    elif name[0] == "M":
                        if n == 0:
                            pe.wait_ge(dlo_ready, GB * g + GB)
                        pe.wait_ge(unit_done, l1_unit("M01" if n < 2 else "M23", g)[3])
                        slot, cols = n // 2, (n % 2) * P
                        product(j, [(w_hi[:, slot, k * 2 * P + cols:k * 2 * P + cols + P],
                                     w_lo[:, slot, k * 2 * P + cols:k * 2 * P + cols + P], d_hi[:, k, :], d_lo[:, k, :])
                                    for k in range(GB)])
                    else:
                        slot = {"V0": 0, "V1": 1, "V2": 0, "V3": 1, "G0": 0, "G1": 1, "G2": 1, "G3": 0}[name]
                        if name not in ("V0", "V1"):
                            pe.wait_ge(unit_done, l1_unit(name, g)[3])
                        elif first:
                            pe.wait_ge(unit_done, l0_unit(("xa'", "gc'")[n], HEADS - 1)[3])
                            if n == 0:
                                pe.wait_ge(evacuated[Job(J_BC1).slot], Job(J_BC1).read)
                        else:
                            pe.wait_ge(unit_done, l1_unit(name + "'", g - 1)[3])
                        project(j, slot)

            l1(0, True)
            with pe.Fori(1, GROUPS) as g:
                l1(g, False)
            pe.wait_ge(ylo_ready, 2 * HEADS + GB * GROUPS)
            pe.wait_ge(unit_done, l1_unit("WoD", GROUPS - 1)[3])
            for k in range(KB):
                out_project(Job(J_L1O + k), k)
            pe.wait_ge(ssq_added, 3 * KB)
            column_sums(Job(J_STAT2), vp[:, PAD:], SB)
            for b in range(SB):
                j = Job(J_OUT + b)
                take(j)
                for k in range(KB):
                    ins = nc.tensor.transpose(psum[:, j.slot, k * P:(k + 1) * P], xT[:, k, b * P:(b + 1) * P],
                                              ident[:, :])
                ins.then_inc(psum_full, 1)


_INS = ["x", "c", "norm_g", "mod_w", "mod_b", "hy_w_in", "hy_conv_w", "hy_conv_b", "lru_w_a", "lru_b_a", "lru_w_x",
        "lru_b_x", "lru_lambda", "sc_conv_w", "hy_w_out", "pool_w_in", "pool_w_grp", "pool_b_grp", "pool_scale",
        "pool_w_out", "final_g"]


def kernel(**inputs):
    import numpy as np
    import concourse.bacc as bacc
    from concourse.bass_utils import run_bass_kernel_spmd

    nc = bacc.Bacc("TRN2", target_bir_lowering=False, num_devices=1, dynamic_dma_scratch_size=512)
    arrays, args = {}, []
    for name in _INS:
        a = np.ascontiguousarray(inputs[name])
        arrays[f"in_{name}"] = a
        args.append(nc.dram_tensor(f"in_{name}", a.shape, mybir.dt.from_np(a.dtype), kind="ExternalInput").ap())
    out = nc.dram_tensor("out", arrays["in_x"].shape, F32, kind="ExternalOutput").ap()
    build(nc, *args, out)
    r = run_bass_kernel_spmd(nc, [arrays], core_ids=[0])
    return r.results[0]["out"]
```

```python
from contextlib import ExitStack

import concourse.bass as bass
from concourse import mybir

F32 = mybir.dt.float32
F32R = mybir.dt.float32r
ALU = mybir.AluOpType
ACT = mybir.ActivationFunctionType

P = 128
SLOTS = 4
RAW = 2
HALF = 512
EPS = 1e-6
LRU_C = 8.0
TINY = 2.0 ** -110
WINDOWS = (2, 4, 8, 16)
PAD = max(WINDOWS)

ROWS_A = (("norm_g", 16), ("mod_b", 48), ("conv_w", 32), ("conv_b", 8), ("b_a", 8), ("b_x", 8), ("c", 8))
ROWS_B = (("lam", 8), ("sc_w", 24), ("pool_b", 16), ("pool_scale", 16), ("final_g", 8))
COL = {}
for _name, _n in ROWS_A + ROWS_B:
    COL[_name] = sum(COL[k][1] for k in COL), _n
COL = {k: v[0] for k, v in COL.items()}
NCOL = sum(n for _, n in ROWS_A + ROWS_B)

L0_FIRST = ["xa", "gc", "v", "GM", "r", "i", "ga", "gbp", "gb"]
L0_NEXT = ["xa", "O0", "O1", "gc", "O2", "O3", "v", "O4", "O5", "r", "i", "O6", "O7", "ga", "gbp", "gb"]
L0_UNITS = ["v", "G", "ga", "M0", "gbp", "M1", "WoA", "WoB", "gb", "M2", "xa'", "gc'"]
L0_SPLITS = [u for u in L0_UNITS if u[0] != "M"]
L0_COLS = {"xa": 0, "ga": 1, "gbp": 2, "gc": 3, "v": 4, "gb": 5}

L1_FIRST = ["V0", "V1", "V2", "V3", "G0", "G1", "M0", "M1", "G2", "O0", "O1", "O2", "O3", "G3", "O4", "O5", "O6", "O7",
            "M2", "M3"]
L1_NEXT = ["V0", "Q0", "Q1", "V1", "Q2", "Q3", "V2", "Q4", "Q5", "V3", "Q6", "Q7"] + L1_FIRST[4:]
L1_UNITS = ["V2", "V3", "G0", "G1", "WoA", "WoB", "M01", "G2", "G3", "M23", "WoC", "WoD", "V0'", "V1'"]


class Job:

    def __init__(self, const, turn=0, stride=0):
        self.const, self.turn, self.stride = const, turn, stride
        self.slot = const % SLOTS
        assert stride % SLOTS == 0

    @property
    def full(self):
        return self.turn * self.stride + (self.const + 1)

    @property
    def read(self):
        return self.turn * (self.stride // SLOTS) + (self.const // SLOTS + 1)

    @property
    def free(self):
        return None if self.const < SLOTS and self.stride == 0 else self.turn * (self.stride // SLOTS) + self.const // SLOTS


def build(nc, x, c, norm_g, mod_w, mod_b, hy_w_in, hy_conv_w, hy_conv_b, lru_w_a, lru_b_a, lru_w_x, lru_b_x,
          lru_lambda, sc_conv_w, hy_w_out, pool_w_in, pool_w_grp, pool_b_grp, pool_scale, pool_w_out, final_g, out):
    S, D = x.shape[1:]
    KB = D // P
    SB = S // P
    NH = S // HALF
    HEADS = lru_w_a.shape[1]
    GROUPS = len(WINDOWS)
    GB = pool_w_grp.shape[2] // P
    NMOD = 3 * D
    assert S == D == 1024 and KB == HEADS == 8 and GB == 4 and lru_w_a.shape[2] == P

    J_VEC, J_XT, J_BC0, J_SCALE0, J_SHIFT0 = 0, 1, 1 + KB, 2 + KB, 3 + KB
    J_L0 = J_SHIFT0 + 1
    J_L0N = J_L0 + len(L0_FIRST)
    J_MOD1 = J_L0N + (HEADS - 1) * len(L0_NEXT)
    J_L0O = J_MOD1 + 1
    J_STAT1, J_BC1 = J_L0O + KB, J_L0O + KB + 1
    J_L1 = J_BC1 + 1
    J_L1N = J_L1 + len(L1_FIRST)
    J_L1O = J_L1N + (GROUPS - 1) * len(L1_NEXT)
    J_STAT2 = J_L1O + KB
    J_OUT = J_STAT2 + 1

    def l0_job(name, i, first):
        return Job(J_L0 + L0_FIRST.index(name)) if first else Job(J_L0N + L0_NEXT.index(name), i - 1, len(L0_NEXT))

    def l1_job(name, g, first):
        return Job(J_L1 + L1_FIRST.index(name)) if first else Job(J_L1N + L1_NEXT.index(name), g - 1, len(L1_NEXT))

    def l0_unit(name, i):
        at = 2 + L0_UNITS.index(name)
        return (at % RAW, i * (16 * len(L0_UNITS) // RAW) + 16 * (at // RAW + 1),
                i * len(L0_SPLITS) + (3 + L0_SPLITS.index(name) if name[0] != "M" else 0), i * len(L0_UNITS) + (at + 1))

    U_L1 = 2 + HEADS * len(L0_UNITS)
    N_L1 = 2 + HEADS * len(L0_SPLITS)

    def l1_unit(name, g):
        at = U_L1 + L1_UNITS.index(name)
        return (at % RAW, g * (16 * len(L1_UNITS) // RAW) + 16 * (at // RAW + 1),
                g * len(L1_UNITS) + (N_L1 + 1 + L1_UNITS.index(name)), g * len(L1_UNITS) + (at + 1))

    with ExitStack() as ctx:
        def sb(name, shape, dt=F32, stack=ctx):
            return stack.enter_context(nc.sbuf_tensor(name, shape, dt))

        def sem(name):
            return ctx.enter_context(nc.semaphore(name))

        xT = sb("xT", [P, KB, S])
        h_hi = sb("h_hi", [P, KB, S], F32R)
        h_lo = sb("h_lo", [P, KB, S], F32R)
        w_hi = sb("w_hi", [P, 2, 1024], F32R)
        w_lo = sb("w_lo", [P, 2, 1024], F32R)
        wo_hi = sb("wo_hi", [P, 2, D], F32R)
        wo_lo = sb("wo_lo", [P, 2, D], F32R)
        g_hi = sb("g_hi", [P, 2 * P], F32R)
        g_lo = sb("g_lo", [P, 2 * P], F32R)
        y_hi = sb("y_hi", [P, 2, S], F32R)
        y_lo = sb("y_lo", [P, 2, S], F32R)
        raw = sb("raw", [P, RAW, 1024])
        mod_acc = sb("mod_acc", [P, NMOD])
        vec = sb("vec", [P, NCOL])
        rows_a = sb("rows_a", [P, P])
        rows_b = sb("rows_b", [NCOL - P, P])
        ident = sb("ident", [P, P])
        ones = sb("ones", [P, P])
        modv = sb("modv", [P, 2, 3 * KB])
        gsc = sb("gsc", [P, 2, KB])
        ca = sb("ca", [P, KB])
        sps = sb("sps", [P, 8, HEADS])
        c8 = sb("c8", [P, 2, HEADS])
        cst = sb("cst", [P, 2])
        ss = sb("ss", [P, SB])
        sd = sb("sd", [P, 3, SB])
        rstd = sb("rstd", [P, 3, SB])
        pos = sb("pos", [P, PAD], mybir.dt.int32)
        icnt = sb("icnt", [P, GROUPS, PAD])
        fix = sb("fix", [P, PAD])

        with ExitStack() as phase:
            st0 = sb("st0", [P, 13, S], F32, phase)
        with ExitStack() as phase:
            xc_hi = sb("xc_hi", [P, S], F32R, phase)
            xc_lo = sb("xc_lo", [P, S], F32R, phase)
            scr = sb("scr", [P, 11, S], F32, phase)
        with ExitStack() as phase:
            d_hi = sb("d_hi", [P, GB, S], F32R, phase)
            d_lo = sb("d_lo", [P, GB, S], F32R, phase)
            sg = sb("sg", [P, 2, S], F32, phase)
            vp = sb("vp", [P, PAD + S], F32, phase)
            win = [sb(f"win{n}", [P, PAD + S], F32, phase) for n in range(2)]
        with ExitStack() as phase:
            ob = sb("ob", [P, SB, D], F32, phase)
        XC, GCS, Z, SC, R, G, TH, A, A2, SGA, SGB = (scr[:, n, :] for n in range(11))
        bc_sb = st0[:, SB + 4, :]
        diag0 = mod_acc[:, 2 * D:3 * D]
        x_rows, stage, gate_acc = st0[:, 0:SB, :], st0[:, SB:SB + 4, :], st0[:, SB + 4, :]
        psum = ctx.enter_context(nc.psum_tensor("psum", [P, SLOTS, 1024], F32))

        rows_in = sem("rows_in")
        x_in = [sem(f"x_in{b}") for b in range(SB)]
        stage_in = [sem(f"stage_in{n}") for n in range(4)]
        raw_in = [sem(f"raw_in{n}") for n in range(RAW)]
        gate_x_in = sem("gate_x_in")
        out_done = sem("out_done")
        const_step = sem("const_step")
        psum_full = sem("psum_full")
        evacuated = [sem(f"evacuated{n}") for n in range(SLOTS)]
        hi_done = sem("hi_done")
        unit_done = sem("unit_done")
        small = sem("small")
        ca_sig = sem("ca_sig")
        lam_exp = sem("lam_exp")
        stage_used = sem("stage_used")
        mod_zero = sem("mod_zero")
        ss_ready = sem("ss_ready")
        rstd_ready = sem("rstd_ready")
        xg_ready = sem("xg_ready")
        sq_ready = sem("sq_ready")
        ssq_added = sem("ssq_added")
        sd_ready = sem("sd_ready")
        diag_ready = sem("diag_ready")
        xn_ready = sem("xn_ready")
        hx_ready = sem("hx_ready")
        hhi_ready = sem("hhi_ready")
        h_ready = sem("h_ready")
        modv_ready = sem("modv_ready")
        conv0 = sem("conv0")
        conv_tap = sem("conv_tap")
        xc_hi_ready = sem("xc_hi_ready")
        xc_ready = sem("xc_ready")
        sc0 = sem("sc0")
        sc_tap = sem("sc_tap")
        gx_done = sem("gx_done")
        th_ready = sem("th_ready")
        a_ready = sem("a_ready")
        a2_ready = sem("a2_ready")
        m2_done = sem("m2_done")
        m_ready = sem("m_ready")
        m_reset = sem("m_reset")
        u_done = sem("u_done")
        scan_done = sem("scan_done")
        sga_ready = sem("sga_ready")
        sgb_ready = sem("sgb_ready")
        y_ready = sem("y_ready")
        yhi_ready = sem("yhi_ready")
        ylo_ready = sem("ylo_ready")
        win_step = sem("win_step")
        d_ready = sem("d_ready")
        dhi_ready = sem("dhi_ready")
        dlo_ready = sem("dlo_ready")
        sg_ready = sem("sg_ready")
        pads = sem("pads")

        def v(name, n=0, count=1):
            return vec[:, bass.ds(COL[name] + n, count)]

        def parameter_rows(engine, params):
            for name, src in params:
                n = dict(ROWS_A + ROWS_B)[name]
                dst = rows_a[COL[name]:COL[name] + n, :] if COL[name] < P else rows_b[COL[name] - P:COL[name] - P + n, :]
                outer = " ".join("abc"[:len(src.shape) - 1])
                flat = src.rearrange(f"{outer} (r q) -> ({outer} r) q", q=P)
                engine.dma_start(dst, flat).then_inc(rows_in, 16)

        block = ctx.enter_context(nc.Block())

        @block.sync
        def _(sp):
            parameter_rows(sp, (("mod_b", mod_b), ("conv_w", hy_conv_w), ("conv_b", hy_conv_b), ("b_a", lru_b_a),
                                ("b_x", lru_b_x), ("norm_g", norm_g)))
            for b in range(SB):
                sp.dma_start(x_rows[:, b, :], x[0, b * P:(b + 1) * P, :]).then_inc(x_in[b], 16)

            def stage_load(slot, k, chunk):
                sp.dma_start(stage[:, slot, :], mod_w[0][bass.ds(k * P, P), chunk * D:(chunk + 1) * D])\
                  .then_inc(stage_in[slot], 16)

            def raw_load(at, src, blocks):
                sp.dma_start(raw[:, at, :].rearrange("p (k n) -> p k n", k=blocks), src).then_inc(raw_in[at], 16)

            hy_in = hy_w_in[0].rearrange("(k p) n -> p k n", p=P)
            pool_in = pool_w_in[0].rearrange("(k p) n -> p k n", p=P)

            for slot in range(4):
                stage_load(slot, slot, 1)
            for slot in range(4):
                sp.wait_ge(stage_used, slot + 2)
                stage_load(slot, 4 + slot, 1)
            with sp.Fori(0, KB // 4) as t:
                for slot in range(4):
                    sp.wait_ge(stage_used, 4 * t + (KB - 4 + slot + 2))
                    stage_load(slot, 4 * t + slot, 0)
            raw_load(0, hy_in[:, :, L0_COLS["xa"] * D:L0_COLS["xa"] * D + P], KB)
            raw_load(1, hy_in[:, :, L0_COLS["gc"] * D:L0_COLS["gc"] * D + P], KB)
            for k in range(KB):
                sp.wait_ge(stage_used, 2 * KB - 2 + k)
                stage_load(k % 4, k, 2)

            def l0_loads(i, last):
                for name in L0_UNITS:
                    at, _, _, done = l0_unit(name, i)
                    sp.wait_ge(unit_done, done - RAW)
                    if name == "G":
                        sp.dma_start(raw[:, at, 0:P], lru_w_a[0][i]).then_inc(raw_in[at], 16)
                        sp.dma_start(raw[:, at, P:2 * P], lru_w_x[0][i]).then_inc(gate_x_in, 16)
                    elif name[0] == "M":
                        chunk = int(name[1])
                        raw_load(at, mod_w[1][bass.ds(i * P, P), chunk * D:(chunk + 1) * D]
                                 .rearrange("p (k n) -> p k n", k=1), 1)
                    elif name in ("WoA", "WoB"):
                        raw_load(at, hy_w_out[0][bass.ds(i * P + (D if name == "WoB" else 0), P), :]
                                 .rearrange("p (k n) -> p k n", k=1), 1)
                    elif name[-1] != "'":
                        raw_load(at, hy_in[:, :, bass.ds(i * P + L0_COLS[name] * D, P)], KB)
                    elif not last:
                        raw_load(at, hy_in[:, :, bass.ds((i + 1) * P + L0_COLS[name[:-1]] * D, P)], KB)
                    else:
                        n = ("xa'", "gc'").index(name)
                        raw_load(at, pool_in[:, :, n * P:(n + 1) * P], KB)

            with sp.Fori(0, HEADS - 1) as i:
                l0_loads(i, False)
            l0_loads(HEADS - 1, True)

            def l1_loads(g, last):
                for name in L1_UNITS:
                    if last and name[-1] == "'":
                        continue
                    at, _, _, done = l1_unit(name, g)
                    sp.wait_ge(unit_done, done - RAW)
                    if name[0] == "V":
                        turn = (g + 1) if name[-1] == "'" else g
                        raw_load(at, pool_in[:, :, bass.ds(turn * (GB * P) + int(name[1]) * P, P)], KB)
                    elif name[0] == "G":
                        raw_load(at, pool_in[:, :, bass.ds(g * (GB * P) + (2 * D + int(name[1]) * P), P)], KB)
                    elif name[0] == "M":
                        n = int(name[1]) * P
                        raw_load(at, pool_w_grp[0][g].rearrange("(k p) n -> p k n", p=P)[:, :, n:n + 2 * P], GB)
                    else:
                        raw_load(at, pool_w_out[0][bass.ds(g * (GB * P) + "ABCD".index(name[2]) * P, P), :]
                                 .rearrange("p (k n) -> p k n", k=1), 1)

            with sp.Fori(0, GROUPS - 1) as g:
                l1_loads(g, False)
            l1_loads(GROUPS - 1, True)

            for b in range(SB):
                j = Job(J_OUT + b)
                sp.wait_ge(evacuated[j.slot], j.read)
                sp.dma_start(out[0, b * P:(b + 1) * P, :], ob[:, b, :]).then_inc(out_done, 16)
            sp.wait_ge(out_done, 16 * SB)

        SIG_AT = 2
        CONSTS = 6

        @block.gpsimd
        def _(pool):
            nc.gpsimd.memset(ident[:, :], 0.0).then_inc(const_step, 1)
            nc.gpsimd.memset(ones[:, :], 1.0).then_inc(const_step, 1)
            nc.gpsimd.memset(cst[:, 0:1], EPS).then_inc(const_step, 1)
            nc.gpsimd.memset(cst[:, 1:2], TINY).then_inc(const_step, 1)
            nc.gpsimd.iota(pos[:, :], [[1, PAD]], base=1, channel_multiplier=0).then_inc(const_step, 1)
            pool.wait_ge(const_step, 5)
            nc.gpsimd.affine_select(out=ident[:, :], in_=ident[:, :], compare_op=ALU.not_equal, fill=1.0, base=0,
                                    pattern=[[-1, P]], channel_multiplier=1).then_inc(const_step, 1)
            nc.gpsimd.memset(mod_acc[:, 0:2 * D], 0.0).then_inc(stage_used, 1)
            pool.wait_ge(evacuated[Job(J_BC0).slot], Job(J_BC0).read)
            for k in range(KB):
                nc.gpsimd.tensor_tensor(x_rows[:, k, :], xT[:, k, :], bc_sb, ALU.mult).then_inc(xn_ready, 1)
            pool.wait_ge(psum_full, Job(J_SHIFT0).full)
            nc.gpsimd.memset(mod_acc[:, :], 0.0).then_inc(mod_zero, 1)

        @block.scalar
        def _(act):
            parameter_rows(act, (("c", c), ("lam", lru_lambda), ("sc_w", sc_conv_w), ("pool_b", pool_b_grp),
                                 ("pool_scale", pool_scale), ("final_g", final_g)))

            def split_hi(dst, unit, n=1024, second=None):
                slot, landed, _, _ = unit
                act.wait_ge(raw_in[slot], landed)
                if second is not None:
                    act.wait_ge(gate_x_in, second)
                nc.scalar.activation(dst, raw[:, slot, 0:n], ACT.Copy).then_inc(hi_done, 1)

            def squares(k, turn, sq):
                if k >= 2:
                    act.wait_ge(ssq_added, (turn - 1) * (KB - 1) + k - 1)
                nc.scalar.activation(sq[k % 2], xT[:, k, :], ACT.Square).then_inc(sq_ready, 1)

            def root(turn, job):
                act.wait_ge(psum_full, job.full)
                nc.scalar.activation(sd[:, turn, :], psum[:, job.slot, 0:SB], ACT.Sqrt, scale=1.0 / D,
                                     bias=cst[:, 0:1]).then_inc(sd_ready, 1)

            def modulate(turn, hx):
                for k in range(KB):
                    n = turn * KB + k
                    if turn and k == KB - 1:
                        act.wait_ge(evacuated[Job(J_BC1).slot], Job(J_BC1).read)
                    else:
                        act.wait_ge(xn_ready, n + 1)
                    nc.scalar.activation(hx[k % len(hx)], hx[k % len(hx)], ACT.Identity, scale=gsc[:, turn, k:k + 1],
                                         bias=modv[:, turn, k:k + 1]).then_inc(hx_ready, 1)
                    act.wait_ge(hx_ready, n + 1)
                    nc.scalar.activation(h_hi[:, k, :], hx[k % len(hx)], ACT.Copy).then_inc(hhi_ready, 1)

            for b in range(SB):
                if b == SIG_AT:
                    act.wait_ge(small, 2)
                    nc.scalar.activation(ca[:, :], v("c", 0, KB), ACT.Sigmoid).then_inc(ca_sig, 1)
                    nc.scalar.activation(sps[:, 1, :], sps[:, 0, :], ACT.Exp).then_inc(lam_exp, 1)
                act.wait_ge(x_in[b], 16)
                if b >= 2:
                    act.wait_ge(ss_ready, b - 1)
                nc.scalar.activation(y_hi[:, b % 2, :], x_rows[:, b, :], ACT.Square, accum_out=ss[:, b:b + 1])\
                  .then_inc(ss_ready, 1)
            act.wait_ge(ss_ready, SB)
            act.wait_ge(const_step, CONSTS)
            nc.scalar.activation(sd[:, 0, :], ss[:, :], ACT.Sqrt, scale=1.0 / D, bias=cst[:, 0:1]).then_inc(sd_ready, 1)
            for k in range(KB):
                j = Job(J_XT + k)
                act.wait_ge(psum_full, j.full)
                nc.scalar.activation(xT[:, k, :], psum[:, j.slot, :], ACT.Copy).then_inc(evacuated[j.slot], 1)
            j = Job(J_BC0)
            act.wait_ge(psum_full, j.full)
            act.wait_ge(evacuated[Job(J_XT + KB - 1).slot], Job(J_XT + KB - 1).read)
            nc.scalar.activation(bc_sb, psum[:, j.slot, :], ACT.Copy).then_inc(evacuated[j.slot], 1)
            split_hi(w_hi[:, 0, :], (0, 16, None, None))
            split_hi(w_hi[:, 1, :], (1, 16, None, None))
            act.wait_ge(modv_ready, 1)
            modulate(0, [x_rows[:, k, :] for k in range(KB)])

            def l0(i, first):
                def job(name):
                    return l0_job(name, i, first)

                act.wait_ge(psum_full, job("xa").full)
                split_hi(w_hi[:, 0, :], l0_unit("v", i))
                if not first:
                    act.wait_ge(gx_done, i)
                nc.scalar.activation(XC, psum[:, job("xa").slot, :], ACT.Identity, scale=v("conv_w", 3 * HEADS + i),
                                     bias=v("conv_b", i)).then_inc(conv0, 1)
                split_hi(g_hi[:, :], l0_unit("G", i), 2 * P, 16 * (i + 1))
                act.wait_ge(evacuated[job("xa").slot], job("xa").read)
                nc.scalar.activation(xc_hi[:, :], XC, ACT.Copy).then_inc(xc_hi_ready, 1)
                act.wait_ge(psum_full, job("gc").full)
                split_hi(w_hi[:, 1, :], l0_unit("ga", i))
                nc.scalar.activation(GCS, psum[:, job("gc").slot, :], ACT.Copy).then_inc(evacuated[job("gc").slot], 1)
                act.wait_ge(psum_full, job("v").full)
                split_hi(w_hi[:, 0, :], l0_unit("gbp", i))
                act.wait_ge(evacuated[job("v").slot], job("v").read)
                if not first:
                    act.wait_ge(y_ready, 2 * i)
                nc.scalar.activation(SC, Z, ACT.Copy, scale=v("sc_w", 2 * HEADS + i)).then_inc(sc0, 1)
                act.wait_ge(psum_full, job("r").full)
                nc.scalar.activation(R, psum[:, job("r").slot, :], ACT.Sigmoid, bias=v("b_a", i))\
                  .then_inc(evacuated[job("r").slot], 1)
                act.wait_ge(psum_full, job("i").full)
                nc.scalar.activation(G, psum[:, job("i").slot, :], ACT.Sigmoid, bias=v("b_x", i))\
                  .then_inc(evacuated[job("i").slot], 1)
                act.wait_ge(evacuated[job("r").slot], job("r").read)
                nc.scalar.activation(TH, R, ACT.Tanh, scale=c8[:, 0, bass.ds(i, 1)]).then_inc(th_ready, 1)
                nc.scalar.activation(A, R, ACT.Exp, scale=c8[:, 1, bass.ds(i, 1)]).then_inc(a_ready, 1)
                act.wait_ge(a_ready, i + 1)
                nc.scalar.activation(A2, A, ACT.Square).then_inc(a2_ready, 1)
                act.wait_ge(m2_done, i + 1)
                nc.scalar.activation(A2, TH, ACT.Sqrt, bias=cst[:, 1:2]).then_inc(m_ready, 1)
                if not first:
                    act.wait_ge(psum_full, job("O7").full)
                split_hi(wo_hi[:, 0, :], l0_unit("WoA", i))
                split_hi(wo_hi[:, 1, :], l0_unit("WoB", i))
                act.wait_ge(psum_full, job("ga").full)
                split_hi(w_hi[:, 1, :], l0_unit("gb", i))
                nc.scalar.activation(SGA, psum[:, job("ga").slot, :], ACT.Sigmoid).then_inc(sga_ready, 1)
                act.wait_ge(psum_full, job("gbp").full)
                split_hi(w_hi[:, 0, :], l0_unit("xa'", i))
                act.wait_ge(y_ready, 2 * i + 1)
                nc.scalar.activation(y_hi[:, 0, :], SGA, ACT.Copy).then_inc(yhi_ready, 1)
                act.wait_ge(psum_full, job("gb").full)
                split_hi(w_hi[:, 1, :], l0_unit("gc'", i))
                nc.scalar.activation(SGB, psum[:, job("gb").slot, :], ACT.Sigmoid).then_inc(sgb_ready, 1)
                act.wait_ge(y_ready, 2 * i + 2)
                nc.scalar.activation(y_hi[:, 1, :], SGB, ACT.Copy).then_inc(yhi_ready, 1)

            l0(0, True)
            with act.Fori(1, HEADS) as i:
                l0(i, False)

            for k in range(KB):
                act.wait_ge(evacuated[Job(J_L0O + k).slot], Job(J_L0O + k).read)
                squares(k, 1, (scr[:, 0, :], scr[:, 1, :]))
            root(1, Job(J_STAT1))
            act.wait_ge(modv_ready, 2)
            modulate(1, [scr[:, 4 + n, :] for n in range(4)])

            def l1(g, first, last):
                def job(name):
                    return l1_job(name, g, first)

                def unit(name):
                    return l1_unit(name, g)

                def pair_y(n):
                    for m in range(2):
                        j = job(f"M{n + m}")
                        act.wait_ge(evacuated[j.slot], j.read)
                        nc.scalar.activation(y_hi[:, m, :], sg[:, m, :], ACT.Copy).then_inc(yhi_ready, 1)

                def gates(n):
                    j = job(f"G{n}")
                    act.wait_ge(ylo_ready, GB * g + (2 * HEADS + n - 1))
                    nc.scalar.activation(sg[:, n % 2, :], psum[:, j.slot, :], ACT.Sigmoid).then_inc(sg_ready, 1)

                for n in range(GB):
                    j = job(f"V{n}")
                    act.wait_ge(psum_full, j.full)
                    split_hi(w_hi[:, n % 2, :], unit(("V2", "V3", "G0", "G1")[n]))
                    if n or not first:
                        act.wait_ge(dlo_ready, GB * g + n)
                    nc.scalar.activation(vp[:, PAD:], psum[:, j.slot, :], ACT.Copy).then_inc(evacuated[j.slot], 1)
                    act.wait_ge(d_ready, GB * g + (n + 1))
                    nc.scalar.activation(d_hi[:, n, :], vp[:, PAD:], ACT.Copy).then_inc(dhi_ready, 1)
                if not first:
                    act.wait_ge(psum_full, job("Q7").full)
                split_hi(wo_hi[:, 0, :], unit("WoA"))
                split_hi(wo_hi[:, 1, :], unit("WoB"))
                act.wait_ge(psum_full, job("G0").full)
                split_hi(w_hi[:, 0, :], unit("M01"))
                gates(0)
                act.wait_ge(psum_full, job("G1").full)
                split_hi(w_hi[:, 1, :], unit("G2"))
                gates(1)
                act.wait_ge(psum_full, job("M1").full)
                split_hi(w_hi[:, 0, :], unit("G3"))
                pair_y(0)
                act.wait_ge(psum_full, job("G2").full)
                split_hi(w_hi[:, 1, :], unit("M23"))
                gates(2)
                act.wait_ge(psum_full, job("G3").full)
                gates(3)
                act.wait_ge(psum_full, job("O7").full)
                split_hi(wo_hi[:, 0, :], unit("WoC"))
                split_hi(wo_hi[:, 1, :], unit("WoD"))
                if not last:
                    split_hi(w_hi[:, 0, :], unit("V0'"))
                act.wait_ge(psum_full, job("M3").full)
                if not last:
                    split_hi(w_hi[:, 1, :], unit("V1'"))
                pair_y(2)

            l1(0, True, False)
            with act.Fori(1, GROUPS - 1) as g:
                l1(g, False, False)
            l1(GROUPS - 1, False, True)

            for k in range(KB):
                act.wait_ge(evacuated[Job(J_L1O + k).slot], Job(J_L1O + k).read)
                if k == 0:
                    act.wait_ge(ylo_ready, 2 * HEADS + GB * GROUPS)
                squares(k, 2, (sg[:, 0, :], sg[:, 1, :]))
                nc.scalar.activation(xT[:, k, :], xT[:, k, :], ACT.Copy, scale=v("final_g", k)).then_inc(xg_ready, 1)
            root(2, Job(J_STAT2))
            act.wait_ge(evacuated[Job(J_STAT2).slot], Job(J_STAT2).read)
            for b in range(0, SB, 2):
                j = Job(J_OUT + b)
                act.wait_ge(psum_full, j.full)
                nc.scalar.activation(ob[:, b, :], psum[:, j.slot, :], ACT.Copy, scale=rstd[:, 2, b:b + 1])\
                  .then_inc(evacuated[j.slot], 1)

        @block.vector
        def _(dve):
            smalls = [0]

            def step(ins):
                smalls[0] += 1
                ins.then_inc(small, 1)
                dve.wait_ge(small, smalls[0])

            def split_lo(dst, hi, unit, n=1024):
                slot, _, done, _ = unit
                dve.wait_ge(hi_done, done)
                nc.vector.tensor_tensor(dst, raw[:, slot, 0:n], hi.bitcast(F32), ALU.subtract).then_inc(unit_done, 1)

            j = Job(J_VEC)
            dve.wait_ge(psum_full, j.full)
            nc.vector.tensor_copy(vec[:, :], psum[:, j.slot, 0:NCOL]).then_inc(evacuated[j.slot], 1)
            dve.wait_ge(evacuated[j.slot], j.read)
            step(nc.vector.tensor_scalar(sps[:, 0, :], v("lam", 0, HEADS), -1.0, None, ALU.mult))
            step(nc.vector.tensor_tensor(sps[:, 0, :], sps[:, 0, :], v("lam", 0, HEADS), ALU.min))
            dve.wait_ge(ca_sig, 1)
            step(nc.vector.tensor_tensor(ca[:, :], ca[:, :], v("c", 0, KB), ALU.mult))

            def add_unit(dst, src, k, signal):
                nc.vector.scalar_tensor_tensor(out=dst, in0=src, scalar=ca[:, bass.ds(k, 1)], in1=dst, op0=ALU.mult,
                                               op1=ALU.add).then_inc(signal, 1)

            def modulation(layer, blocks, job):
                lo, hi = blocks
                dve.wait_ge(psum_full, job.full)
                at = COL["mod_b"] + layer * 3 * KB
                nc.vector.tensor_tensor(modv[:, layer, lo:hi], psum[:, job.slot, 0:hi - lo],
                                        vec[:, at + lo:at + hi], ALU.add).then_inc(evacuated[job.slot], 1)

            def scale_norm(layer, job):
                dve.wait_ge(evacuated[job.slot], job.read)
                nc.vector.scalar_tensor_tensor(out=gsc[:, layer, :], in0=modv[:, layer, KB:2 * KB], scalar=1.0,
                                               in1=vec[:, COL["norm_g"] + layer * KB:COL["norm_g"] + (layer + 1) * KB],
                                               op0=ALU.add, op1=ALU.mult).then_inc(modv_ready, 1)

            def sum_squares(k, turn, sq, ssq):
                dve.wait_ge(sq_ready, (turn - 1) * KB + k + 1)
                if k == 0:
                    ins = nc.vector.tensor_copy(ssq, sq[0])
                else:
                    dve.wait_ge(ssq_added, (turn - 1) * (KB - 1) + k)
                    ins = nc.vector.tensor_tensor(ssq, ssq, sq[k % 2], ALU.add)
                ins.then_inc(ssq_added, 1)

            def inverse(turn, job):
                dve.wait_ge(sd_ready, turn + 1)
                done, value = (evacuated[job.slot], job.read) if job else (rstd_ready, 1)
                nc.vector.reciprocal(rstd[:, turn, :], sd[:, turn, :]).then_inc(done, 1)
                dve.wait_ge(done, value)

            def diagonals(turn, diag):
                for b in range(SB):
                    ins = nc.vector.tensor_scalar(diag[:, b * P:(b + 1) * P], ident[:, :], rstd[:, turn, b:b + 1], None,
                                                  ALU.mult)
                ins.then_inc(diag_ready, 1)

            def h_low(k, turn, hx):
                dve.wait_ge(hhi_ready, turn * KB + k + 1)
                nc.vector.tensor_tensor(h_lo[:, k, :], hx[k % len(hx)], h_hi[:, k, :].bitcast(F32), ALU.subtract)\
                  .then_inc(h_ready, 1)

            def normalize(turn, job, hx):
                dve.wait_ge(psum_full, job.full)
                for k in range(KB + 2):
                    if k < KB:
                        if k >= 4:
                            dve.wait_ge(h_ready, turn * KB + k - 3)
                        nc.vector.tensor_tensor(hx[k % 4], xT[:, k, :], psum[:, job.slot, :], ALU.mult)\
                          .then_inc(xn_ready if k < KB - 1 else evacuated[job.slot], 1)
                    if k >= 2:
                        h_low(k - 2, turn, hx)

            E_, S_, S2, T_, M_ = (sps[:, n, :] for n in (1, 2, 3, 4, 5))
            TERMS = 9

            def softplus_start():
                dve.wait_ge(lam_exp, 1)
                step(nc.vector.tensor_scalar(T_, E_, 2.0, None, ALU.add))
                step(nc.vector.reciprocal(S_, T_))
                step(nc.vector.tensor_tensor(S_, S_, E_, ALU.mult))
                step(nc.vector.tensor_tensor(S2, S_, S_, ALU.mult))
                step(nc.vector.tensor_scalar(T_, S2, 1.0 / (2 * TERMS + 1), 1.0 / (2 * TERMS - 1), ALU.mult, ALU.add))

            def softplus_term(n):
                step(nc.vector.tensor_tensor(T_, T_, S2, ALU.mult))
                step(nc.vector.tensor_scalar(T_, T_, 1.0 / (2 * n + 1), None, ALU.add))

            def softplus_end():
                step(nc.vector.tensor_tensor(T_, T_, S_, ALU.mult))
                step(nc.vector.tensor_scalar(M_, v("lam", 0, HEADS), -1.0, 0.0, ALU.mult, ALU.max))
                step(nc.vector.scalar_tensor_tensor(out=M_, in0=T_, scalar=2.0, in1=M_, op0=ALU.mult, op1=ALU.add))
                step(nc.vector.tensor_scalar(c8[:, 0, :], M_, LRU_C, None, ALU.mult))
                step(nc.vector.tensor_scalar(c8[:, 1, :], M_, -LRU_C, None, ALU.mult))

            def window_counts(n):
                step(nc.vector.tensor_scalar(icnt[:, n, :], fix[:, :], float(WINDOWS[n]), None, ALU.min))
                step(nc.vector.reciprocal(icnt[:, n, :], icnt[:, n, :]))

            for n, chunk in enumerate((1, 0)):
                with dve.Fori(0, KB // 4) as t:
                    for slot in range(4):
                        dve.wait_ge(stage_in[slot], 16 * t + 16 * (n * (KB // 4) + 1))
                        dve.wait_ge(stage_used, 4 * t + (n * KB + slot + 1))
                        add_unit(mod_acc[:, chunk * D:(chunk + 1) * D], stage[:, slot, :], 4 * t + slot, stage_used)
                if chunk == 1:
                    inverse(0, None)
                    dve.wait_ge(const_step, CONSTS)
                    diagonals(0, diag0)
            split_lo(w_lo[:, 0, :], w_hi[:, 0, :], (0, None, 1, None))
            split_lo(w_lo[:, 1, :], w_hi[:, 1, :], (1, None, 2, None))
            modulation(0, (KB, 2 * KB), Job(J_SCALE0))
            modulation(0, (0, KB), Job(J_SHIFT0))
            dve.wait_ge(evacuated[Job(J_SCALE0).slot], Job(J_SCALE0).read)
            scale_norm(0, Job(J_SHIFT0))
            for k in range(KB):
                if k == 0:
                    softplus_start()
                else:
                    softplus_term(TERMS - 1 - k)
                h_low(k, 0, [x_rows[:, n, :] for n in range(KB)])
                dve.wait_ge(stage_in[k % 4], 16 * (2 * KB // 4 + k // 4 + 1))
                if k == 0:
                    dve.wait_ge(xn_ready, KB)
                    nc.vector.tensor_scalar(gate_acc, stage[:, 0, :], ca[:, 0:1], None, ALU.mult).then_inc(stage_used, 1)
                else:
                    dve.wait_ge(stage_used, 2 * KB + k + 1)
                    add_unit(gate_acc, stage[:, k % 4, :], k, stage_used)
            softplus_term(0)
            softplus_end()

            def residual(k, layer, job):
                dve.wait_ge(psum_full, job.full)
                nc.vector.scalar_tensor_tensor(out=xT[:, k, :], in0=psum[:, job.slot, :],
                                               scalar=modv[:, layer, 2 * KB + k:2 * KB + k + 1], in1=xT[:, k, :],
                                               op0=ALU.mult, op1=ALU.add).then_inc(evacuated[job.slot], 1)

            def add_mod(i, chunk):
                slot, landed, _, done = l0_unit(f"M{chunk}", i)
                dve.wait_ge(raw_in[slot], landed)
                dve.wait_ge(unit_done, done - 1)
                add_unit(mod_acc[:, chunk * D:(chunk + 1) * D], raw[:, slot, :], i, unit_done)

            def l0(i, first):
                def job(name):
                    return l0_job(name, i, first)

                def outs(*blocks):
                    if not first:
                        for k in blocks:
                            residual(k, 0, job(f"O{k}"))

                split_lo(w_lo[:, 0, :], w_hi[:, 0, :], l0_unit("v", i))
                xa = job("xa")
                dve.wait_ge(conv0, i + 1)
                for n, back in enumerate((1, 2, 3)):
                    if n:
                        dve.wait_ge(conv_tap, 2 * i + n)
                    nc.vector.scalar_tensor_tensor(out=XC[:, back:], in0=psum[:, xa.slot, 0:S - back],
                                                   scalar=v("conv_w", (3 - back) * HEADS + i), in1=XC[:, back:],
                                                   op0=ALU.mult, op1=ALU.add)\
                      .then_inc(conv_tap if n < 2 else evacuated[xa.slot], 1)
                split_lo(g_lo[:, :], g_hi[:, :], l0_unit("G", i), 2 * P)
                outs(0, 1)
                dve.wait_ge(xc_hi_ready, i + 1)
                nc.vector.tensor_tensor(xc_lo[:, :], XC, xc_hi[:, :].bitcast(F32), ALU.subtract).then_inc(xc_ready, 1)
                split_lo(w_lo[:, 1, :], w_hi[:, 1, :], l0_unit("ga", i))
                if first:
                    dve.wait_ge(mod_zero, 1)
                add_mod(i, 0)
                outs(2, 3)
                split_lo(w_lo[:, 0, :], w_hi[:, 0, :], l0_unit("gbp", i))
                gc, vj = job("gc"), job("v")
                dve.wait_ge(evacuated[gc.slot], gc.read)
                dve.wait_ge(psum_full, vj.full)
                nc.vector.tensor_tensor(Z, psum[:, vj.slot, :], GCS, ALU.mult).then_inc(evacuated[vj.slot], 1)
                add_mod(i, 1)
                outs(4)
                dve.wait_ge(sc0, i + 1)
                for n, back in enumerate((1, 2)):
                    if n:
                        dve.wait_ge(sc_tap, 2 * i + 1)
                    nc.vector.scalar_tensor_tensor(out=SC[:, back:], in0=Z[:, 0:S - back],
                                                   scalar=v("sc_w", (2 - back) * HEADS + i), in1=SC[:, back:],
                                                   op0=ALU.mult, op1=ALU.add).then_inc(sc_tap, 1)
                outs(5)
                if first:
                    modulation(0, (2 * KB, 3 * KB), job("GM"))
                    dve.wait_ge(evacuated[job("GM").slot], job("GM").read)
                ij = job("i")
                dve.wait_ge(evacuated[ij.slot], ij.read)
                nc.vector.tensor_tensor(G, G, XC, ALU.mult).then_inc(gx_done, 1)
                dve.wait_ge(th_ready, i + 1)
                dve.wait_ge(a2_ready, i + 1)
                nc.vector.scalar_tensor_tensor(out=TH, in0=A2, scalar=1.0, in1=TH, op0=ALU.add, op1=ALU.mult)\
                  .then_inc(m2_done, 1)
                outs(6, 7)
                dve.wait_ge(m_ready, i + 1)
                nc.vector.memset(A2[:, 0:1], 1.0).then_inc(m_reset, 1)
                dve.wait_ge(m_reset, i + 1)
                dve.wait_ge(gx_done, i + 1)
                nc.vector.tensor_tensor(G, G, A2, ALU.mult).then_inc(u_done, 1)
                dve.wait_ge(u_done, i + 1)
                nc.vector.tensor_tensor_scan(R, A, G, 0.0, ALU.mult, ALU.add).then_inc(scan_done, 1)
                split_lo(wo_lo[:, 0, :], wo_hi[:, 0, :], l0_unit("WoA", i))
                split_lo(wo_lo[:, 1, :], wo_hi[:, 1, :], l0_unit("WoB", i))
                split_lo(w_lo[:, 1, :], w_hi[:, 1, :], l0_unit("gb", i))
                ga = job("ga")
                dve.wait_ge(sga_ready, i + 1)
                nc.vector.tensor_tensor(SGA, psum[:, ga.slot, :], SGA, ALU.mult).then_inc(evacuated[ga.slot], 1)
                dve.wait_ge(evacuated[ga.slot], ga.read)
                dve.wait_ge(scan_done, i + 1)
                nc.vector.tensor_tensor(SGA, SGA, R, ALU.mult).then_inc(y_ready, 1)
                add_mod(i, 2)
                split_lo(w_lo[:, 0, :], w_hi[:, 0, :], l0_unit("xa'", i))
                gbp = job("gbp")
                dve.wait_ge(psum_full, gbp.full)
                dve.wait_ge(sc_tap, 2 * i + 2)
                nc.vector.tensor_tensor(SC, psum[:, gbp.slot, :], SC, ALU.mult).then_inc(evacuated[gbp.slot], 1)
                dve.wait_ge(yhi_ready, 2 * i + 1)
                nc.vector.tensor_tensor(y_lo[:, 0, :], SGA, y_hi[:, 0, :].bitcast(F32), ALU.subtract)\
                  .then_inc(ylo_ready, 1)
                split_lo(w_lo[:, 1, :], w_hi[:, 1, :], l0_unit("gc'", i))
                gb = job("gb")
                dve.wait_ge(sgb_ready, i + 1)
                nc.vector.tensor_tensor(SGB, psum[:, gb.slot, :], SGB, ALU.mult).then_inc(evacuated[gb.slot], 1)
                dve.wait_ge(evacuated[gb.slot], gb.read)
                dve.wait_ge(evacuated[gbp.slot], gbp.read)
                nc.vector.tensor_tensor(SGB, SGB, SC, ALU.mult).then_inc(y_ready, 1)
                dve.wait_ge(yhi_ready, 2 * i + 2)
                nc.vector.tensor_tensor(y_lo[:, 1, :], SGB, y_hi[:, 1, :].bitcast(F32), ALU.subtract)\
                  .then_inc(ylo_ready, 1)

            l0(0, True)
            with dve.Fori(1, HEADS) as i:
                l0(i, False)

            modulation(1, (0, 3 * KB), Job(J_MOD1))
            scale_norm(1, Job(J_MOD1))
            sq, ssq = (scr[:, 0, :], scr[:, 1, :]), scr[:, 2, :]
            for k in range(KB):
                residual(k, 0, Job(J_L0O + k))
                if k:
                    sum_squares(k - 1, 1, sq, ssq)
            inverse(1, Job(J_STAT1))
            diagonals(1, scr[:, 3, :])
            normalize(1, Job(J_BC1), [scr[:, 4 + n, :] for n in range(4)])

            step(nc.vector.tensor_copy(fix[:, :], pos[:, :]))
            for n in range(GROUPS):
                window_counts(n)
            for buf in (vp, *win):
                nc.vector.memset(buf[:, 0:PAD], 0.0).then_inc(pads, 1)
            dve.wait_ge(pads, 3)

            sums = [0]

            def l1(g):
                first = g == 0

                def job(name):
                    return l1_job(name, g, first)

                def unit(name):
                    return l1_unit(name, g)

                def window_step(ins):
                    sums[0] += 1
                    ins.then_inc(win_step, 1)
                    dve.wait_ge(win_step, sums[0])

                def queued(*blocks):
                    if not first:
                        for k in blocks:
                            residual(k, 1, job(f"Q{k}"))

                def outs(*blocks):
                    for k in blocks:
                        residual(k, 1, job(f"O{k}"))

                def pool_block(n):
                    vj = job(f"V{n}")
                    dve.wait_ge(evacuated[vj.slot], vj.read)
                    src, width, turn = vp, 1, 0
                    while width < WINDOWS[g]:
                        dst = win[turn % 2]
                        window_step(nc.vector.tensor_tensor(dst[:, width:], src[:, width:], src[:, 0:PAD + S - width],
                                                            ALU.add))
                        src, width, turn = dst, 2 * width, turn + 1
                    window_step(nc.vector.tensor_tensor(fix[:, :], src[:, PAD:2 * PAD], icnt[:, g, :], ALU.mult))
                    window_step(nc.vector.tensor_tensor(vp[:, PAD:2 * PAD], fix[:, :], vp[:, PAD:2 * PAD], ALU.subtract))
                    nc.vector.scalar_tensor_tensor(out=vp[:, 2 * PAD:], in0=src[:, 2 * PAD:], scalar=1.0 / WINDOWS[g],
                                                   in1=vp[:, 2 * PAD:], op0=ALU.mult, op1=ALU.subtract)\
                      .then_inc(d_ready, 1)

                def pool_lo(n):
                    dve.wait_ge(dhi_ready, GB * g + n + 1)
                    nc.vector.tensor_tensor(d_lo[:, n, :], vp[:, PAD:], d_hi[:, n, :].bitcast(F32), ALU.subtract)\
                      .then_inc(dlo_ready, 1)

                def gates(n):
                    j = job(f"G{n}")
                    dve.wait_ge(sg_ready, GB * g + n + 1)
                    nc.vector.scalar_tensor_tensor(out=sg[:, n % 2, :], in0=psum[:, j.slot, :],
                                                   scalar=v("pool_scale", GB * g + n), in1=sg[:, n % 2, :],
                                                   op0=ALU.mult, op1=ALU.mult).then_inc(evacuated[j.slot], 1)

                def mixed(n):
                    j, gj = job(f"M{n}"), job(f"G{n}")
                    dve.wait_ge(evacuated[gj.slot], gj.read)
                    dve.wait_ge(psum_full, j.full)
                    nc.vector.scalar_tensor_tensor(out=sg[:, n % 2, :], in0=psum[:, j.slot, :],
                                                   scalar=v("pool_b", GB * g + n), in1=sg[:, n % 2, :],
                                                   op0=ALU.add, op1=ALU.mult).then_inc(evacuated[j.slot], 1)

                def mixed_lo(n):
                    dve.wait_ge(yhi_ready, 2 * HEADS + GB * g + n + 1)
                    nc.vector.tensor_tensor(y_lo[:, n % 2, :], sg[:, n % 2, :], y_hi[:, n % 2, :].bitcast(F32),
                                            ALU.subtract).then_inc(ylo_ready, 1)

                for n in range(GB):
                    split_lo(w_lo[:, n % 2, :], w_hi[:, n % 2, :], unit(("V2", "V3", "G0", "G1")[n]))
                    pool_block(n)
                    queued(2 * n, 2 * n + 1)
                    pool_lo(n)
                split_lo(wo_lo[:, 0, :], wo_hi[:, 0, :], unit("WoA"))
                split_lo(wo_lo[:, 1, :], wo_hi[:, 1, :], unit("WoB"))
                split_lo(w_lo[:, 0, :], w_hi[:, 0, :], unit("M01"))
                gates(0)
                split_lo(w_lo[:, 1, :], w_hi[:, 1, :], unit("G2"))
                gates(1)
                mixed(0)
                split_lo(w_lo[:, 0, :], w_hi[:, 0, :], unit("G3"))
                mixed(1)
                mixed_lo(0)
                mixed_lo(1)
                split_lo(w_lo[:, 1, :], w_hi[:, 1, :], unit("M23"))
                gates(2)
                outs(0, 1, 2, 3)
                gates(3)
                outs(4, 5, 6, 7)
                split_lo(wo_lo[:, 0, :], wo_hi[:, 0, :], unit("WoC"))
                split_lo(wo_lo[:, 1, :], wo_hi[:, 1, :], unit("WoD"))
                if g < GROUPS - 1:
                    split_lo(w_lo[:, 0, :], w_hi[:, 0, :], unit("V0'"))
                mixed(2)
                mixed(3)
                if g < GROUPS - 1:
                    split_lo(w_lo[:, 1, :], w_hi[:, 1, :], unit("V1'"))
                mixed_lo(2)
                mixed_lo(3)

            for g in range(GROUPS):
                l1(g)

            sq, ssq = (sg[:, 0, :], sg[:, 1, :]), vp[:, PAD:]
            for k in range(KB):
                residual(k, 1, Job(J_L1O + k))
                if k:
                    sum_squares(k - 1, 2, sq, ssq)
            inverse(2, Job(J_STAT2))
            for b in range(1, SB, 2):
                j = Job(J_OUT + b)
                dve.wait_ge(psum_full, j.full)
                nc.vector.tensor_scalar(ob[:, b, :], psum[:, j.slot, :], rstd[:, 2, b:b + 1], None, ALU.mult)\
                  .then_inc(evacuated[j.slot], 1)

        @block.tensor
        def _(pe):
            def take(job):
                if job.const >= SLOTS or not isinstance(job.turn, int):
                    pe.wait_ge(evacuated[job.slot], job.free)

            def products(dst, whi, wlo, xhi, xlo, first, last):
                for hh in range(NH):
                    cols = slice(hh * HALF, (hh + 1) * HALF)
                    nc.tensor.matmul(dst[:, cols], whi, xhi[:, cols], start=first, stop=False)
                    nc.tensor.matmul(dst[:, cols], whi, xlo[:, cols], start=False, stop=False)
                for hh in range(NH):
                    cols = slice(hh * HALF, (hh + 1) * HALF)
                    ins = nc.tensor.matmul(dst[:, cols], wlo, xhi[:, cols], start=False, stop=last)
                return ins

            def product(job, blocks):
                take(job)
                for n, block in enumerate(blocks):
                    ins = products(psum[:, job.slot, :], *block, n == 0, n == len(blocks) - 1)
                ins.then_inc(psum_full, 1)

            def weights(slot):
                return [(w_hi[:, slot, k * P:(k + 1) * P], w_lo[:, slot, k * P:(k + 1) * P], h_hi[:, k, :],
                         h_lo[:, k, :]) for k in range(KB)]

            def project(job, slot):
                product(job, weights(slot))

            def first_projects(jobs, turn):
                for job in jobs:
                    take(job)
                for k, n in [(k, n) for k in range(KB // 2) for n in range(2)] + \
                            [(k, n) for n in range(2) for k in range(KB // 2, KB)]:
                    pe.wait_ge(h_ready, turn * KB + k + 1)
                    ins = products(psum[:, jobs[n].slot, :], *weights(n)[k], k == 0, k == KB - 1)
                    if k == KB - 1:
                        ins.then_inc(psum_full, 1)

            def out_project(job, k):
                product(job, [(wo_hi[:, m, k * P:(k + 1) * P], wo_lo[:, m, k * P:(k + 1) * P], y_hi[:, m, :],
                               y_lo[:, m, :]) for m in range(2)])

            def column_sums(job, acc, blocks):
                take(job)
                for n in range(blocks):
                    ins = nc.tensor.matmul(psum[:, job.slot, n:n + 1], acc[:, n * P:(n + 1) * P], ones[:, 0:1],
                                           start=True, stop=True)
                ins.then_inc(psum_full, 1)

            def square_sums(job, turn, ssq, last):
                take(job)
                pe.wait_ge(ssq_added, turn * (KB - 1))
                for n, part in enumerate((ssq, last)):
                    if n:
                        pe.wait_ge(sq_ready, turn * KB)
                    for b in range(SB):
                        ins = nc.tensor.matmul(psum[:, job.slot, b:b + 1], part[:, b * P:(b + 1) * P], ones[:, 0:1],
                                               start=n == 0 and b == 0, stop=n == 1, skip_group_check=True)
                ins.then_inc(psum_full, 1)

            def broadcast(job, turn, diag):
                take(job)
                pe.wait_ge(diag_ready, turn + 1)
                for hh in range(NH):
                    cols = slice(hh * HALF, (hh + 1) * HALF)
                    ins = nc.tensor.matmul(psum[:, job.slot, cols], ones[:, :], diag[:, cols], start=True, stop=True)
                ins.then_inc(psum_full, 1)

            pe.wait_ge(const_step, CONSTS)
            pe.wait_ge(rows_in, 16 * (len(ROWS_A) + len(ROWS_B)))
            nc.tensor.transpose(psum[:, J_VEC, 0:P], rows_a[:, :], ident[:, :])
            nc.tensor.transpose(psum[:, J_VEC, P:NCOL], rows_b[:, :], ident[0:NCOL - P, 0:NCOL - P])\
              .then_inc(psum_full, 1)
            for b in range(SB):
                pe.wait_ge(x_in[b], 16)
            for k in range(KB):
                j = Job(J_XT + k)
                take(j)
                for b in range(SB):
                    ins = nc.tensor.transpose(psum[:, j.slot, b * P:(b + 1) * P], x_rows[:, b, k * P:(k + 1) * P],
                                              ident[:, :])
                ins.then_inc(psum_full, 1)

            broadcast(Job(J_BC0), 0, diag0)
            pe.wait_ge(stage_used, KB + 1)
            column_sums(Job(J_SCALE0), mod_acc[:, D:2 * D], KB)
            pe.wait_ge(stage_used, 2 * KB + 1)
            column_sums(Job(J_SHIFT0), mod_acc[:, 0:D], KB)

            def l0(i, first):
                for name in (L0_FIRST if first else L0_NEXT):
                    j = l0_job(name, i, first)
                    if name[0] == "O":
                        k = int(name[1])
                        if k == 0:
                            pe.wait_ge(ylo_ready, 2 * i)
                            pe.wait_ge(unit_done, l0_unit("WoB", i - 1)[3])
                        out_project(j, k)
                    elif name == "GM":
                        pe.wait_ge(stage_used, 3 * KB + 1)
                        column_sums(j, gate_acc, KB)
                    elif name in ("r", "i"):
                        if name == "r":
                            pe.wait_ge(xc_ready, i + 1)
                            pe.wait_ge(unit_done, l0_unit("G", i)[3])
                        at = slice(0, P) if name == "r" else slice(P, 2 * P)
                        product(j, [(g_hi[:, at], g_lo[:, at], xc_hi[:, :], xc_lo[:, :])])
                    else:
                        slot = ("xa", "gc", "v", "ga", "gbp", "gb").index(name) % 2
                        if name not in ("xa", "gc"):
                            pe.wait_ge(unit_done, l0_unit(name, i)[3])
                        elif first:
                            if name == "gc":
                                pe.wait_ge(unit_done, 2)
                                first_projects((Job(J_L0), Job(J_L0 + 1)), 0)
                            continue
                        else:
                            pe.wait_ge(unit_done, l0_unit(name + "'", i - 1)[3])
                        project(j, slot)

            l0(0, True)
            with pe.Fori(1, HEADS) as i:
                l0(i, False)
            pe.wait_ge(unit_done, l0_unit("M2", HEADS - 1)[3])
            column_sums(Job(J_MOD1), mod_acc, 3 * KB)
            pe.wait_ge(ylo_ready, 2 * HEADS)
            pe.wait_ge(unit_done, l0_unit("WoB", HEADS - 1)[3])
            for k in range(KB):
                out_project(Job(J_L0O + k), k)
            square_sums(Job(J_STAT1), 1, scr[:, 2, :], scr[:, (KB - 1) % 2, :])
            broadcast(Job(J_BC1), 1, scr[:, 3, :])

            def l1(g, first):
                for name in (L1_FIRST if first else L1_NEXT):
                    j = l1_job(name, g, first)
                    n = int(name[1])
                    if name[0] in "QO":
                        if n == 0 and name[0] == "Q":
                            pe.wait_ge(ylo_ready, GB * g + 2 * HEADS)
                            pe.wait_ge(unit_done, l1_unit("WoD", g - 1)[3])
                        elif n == 0:
                            pe.wait_ge(ylo_ready, GB * g + (2 * HEADS + 2))
                            pe.wait_ge(unit_done, l1_unit("WoB", g)[3])
                        out_project(j, n)
                    elif name[0] == "M":
                        if n == 0:
                            pe.wait_ge(dlo_ready, GB * g + GB)
                        pe.wait_ge(unit_done, l1_unit("M01" if n < 2 else "M23", g)[3])
                        slot, cols = n // 2, (n % 2) * P
                        product(j, [(w_hi[:, slot, k * 2 * P + cols:k * 2 * P + cols + P],
                                     w_lo[:, slot, k * 2 * P + cols:k * 2 * P + cols + P], d_hi[:, k, :], d_lo[:, k, :])
                                    for k in range(GB)])
                    else:
                        slot = {"V0": 0, "V1": 1, "V2": 0, "V3": 1, "G0": 0, "G1": 1, "G2": 1, "G3": 0}[name]
                        if name not in ("V0", "V1"):
                            pe.wait_ge(unit_done, l1_unit(name, g)[3])
                        elif first:
                            if n:
                                pe.wait_ge(unit_done, l0_unit("gc'", HEADS - 1)[3])
                                first_projects((Job(J_L1), Job(J_L1 + 1)), 1)
                            continue
                        else:
                            pe.wait_ge(unit_done, l1_unit(name + "'", g - 1)[3])
                        project(j, slot)

            l1(0, True)
            with pe.Fori(1, GROUPS) as g:
                l1(g, False)
            pe.wait_ge(ylo_ready, 2 * HEADS + GB * GROUPS)
            pe.wait_ge(unit_done, l1_unit("WoD", GROUPS - 1)[3])
            for k in range(KB):
                out_project(Job(J_L1O + k), k)
            square_sums(Job(J_STAT2), 2, vp[:, PAD:], sg[:, (KB - 1) % 2, :])
            pe.wait_ge(xg_ready, KB)
            for b in range(SB):
                j = Job(J_OUT + b)
                take(j)
                for k in range(KB):
                    ins = nc.tensor.transpose(psum[:, j.slot, k * P:(k + 1) * P], xT[:, k, b * P:(b + 1) * P],
                                              ident[:, :])
                ins.then_inc(psum_full, 1)


_INS = ["x", "c", "norm_g", "mod_w", "mod_b", "hy_w_in", "hy_conv_w", "hy_conv_b", "lru_w_a", "lru_b_a", "lru_w_x",
        "lru_b_x", "lru_lambda", "sc_conv_w", "hy_w_out", "pool_w_in", "pool_w_grp", "pool_b_grp", "pool_scale",
        "pool_w_out", "final_g"]


def kernel(**inputs):
    import numpy as np
    import concourse.bacc as bacc
    from concourse.bass_utils import run_bass_kernel_spmd

    nc = bacc.Bacc("TRN2", target_bir_lowering=False, num_devices=1, dynamic_dma_scratch_size=512)
    arrays, args = {}, []
    for name in _INS:
        a = np.ascontiguousarray(inputs[name])
        arrays[f"in_{name}"] = a
        args.append(nc.dram_tensor(f"in_{name}", a.shape, mybir.dt.from_np(a.dtype), kind="ExternalInput").ap())
    out = nc.dram_tensor("out", arrays["in_x"].shape, F32, kind="ExternalOutput").ap()
    build(nc, *args, out)
    r = run_bass_kernel_spmd(nc, [arrays], core_ids=[0])
    return r.results[0]["out"]
```

```python
from contextlib import ExitStack

import concourse.bass as bass
from concourse import mybir

F32 = mybir.dt.float32
F32R = mybir.dt.float32r
ALU = mybir.AluOpType
ACT = mybir.ActivationFunctionType

P = 128
SLOTS = 4
RAW = 2
HALF = 512
EPS = 1e-6
LRU_C = 8.0
TINY = 2.0 ** -110
WINDOWS = (2, 4, 8, 16)
PAD = max(WINDOWS)

ROWS_A = (("norm_g", 16), ("mod_b", 48), ("conv_w", 32), ("conv_b", 8), ("b_a", 8), ("b_x", 8), ("lam", 8))
ROWS_B = (("sc_w", 24), ("pool_b", 16), ("pool_scale", 16), ("final_g", 8))
COL = {}
for _name, _n in ROWS_A + ROWS_B:
    COL[_name] = sum(COL[k][1] for k in COL), _n
COL = {k: v[0] for k, v in COL.items()}
NCOL = sum(n for _, n in ROWS_A + ROWS_B)

L0_FIRST = ["xa", "gc", "v", "r", "i", "GM", "ga", "gbp", "gb"]
L0_NEXT = ["xa", "O0", "O1", "gc", "O2", "O3", "v", "O4", "O5", "r", "i", "O6", "O7", "ga", "gbp", "gb"]
L0_UNITS = ["v", "G", "ga", "M0", "gbp", "M1", "WoA", "WoB", "gb", "M2", "xa'", "gc'"]
L0_SPLITS = [u for u in L0_UNITS if u[0] != "M"]
L0_COLS = {"xa": 0, "ga": 1, "gbp": 2, "gc": 3, "v": 4, "gb": 5}

L1_FIRST = ["V0", "V1", "V2", "V3", "G0", "G1", "M0", "M1", "G2", "O0", "O1", "O2", "O3", "G3", "O4", "O5", "O6", "O7",
            "M2", "M3"]
L1_NEXT = ["V0", "Q0", "Q1", "V1", "Q2", "Q3", "V2", "Q4", "Q5", "V3", "Q6", "Q7"] + L1_FIRST[4:]
L1_LAST = L1_NEXT[:-6] + ["M2", "M3", "O4", "O5", "O6", "O7"]
L1_UNITS = ["V2", "V3", "G0", "G1", "WoA", "WoB", "M01", "G2", "G3", "M23", "WoC", "WoD", "V0'", "V1'"]


class Job:

    def __init__(self, const, turn=0, stride=0):
        self.const, self.turn, self.stride = const, turn, stride
        self.slot = const % SLOTS
        assert stride % SLOTS == 0

    @property
    def full(self):
        return self.turn * self.stride + (self.const + 1)

    @property
    def read(self):
        return self.turn * (self.stride // SLOTS) + (self.const // SLOTS + 1)

    @property
    def free(self):
        return None if self.const < SLOTS and self.stride == 0 else self.turn * (self.stride // SLOTS) + self.const // SLOTS


def build(nc, x, c, norm_g, mod_w, mod_b, hy_w_in, hy_conv_w, hy_conv_b, lru_w_a, lru_b_a, lru_w_x, lru_b_x,
          lru_lambda, sc_conv_w, hy_w_out, pool_w_in, pool_w_grp, pool_b_grp, pool_scale, pool_w_out, final_g, out):
    S, D = x.shape[1:]
    KB = D // P
    SB = S // P
    NH = S // HALF
    HEADS = lru_w_a.shape[1]
    GROUPS = len(WINDOWS)
    GB = pool_w_grp.shape[2] // P
    NMOD = 3 * D
    assert S == D == 1024 and KB == HEADS == 8 and GB == 4 and lru_w_a.shape[2] == P

    J_C, J_XT = 0, 1
    J_VEC = J_XT + SB
    J_BC0 = J_VEC + 1
    J_MOD0 = J_BC0 + 1
    J_L0 = J_MOD0 + 2
    J_L0N = J_L0 + len(L0_FIRST)
    J_MOD1 = J_L0N + (HEADS - 1) * len(L0_NEXT)
    J_L0O = J_MOD1 + 1
    J_STAT1 = J_L0O + KB
    J_GATE1 = J_STAT1 + 1
    J_BC1 = J_GATE1 + 1
    J_L1 = J_BC1 + 1
    J_L1N = J_L1 + len(L1_FIRST)
    J_L1O = J_L1N + (GROUPS - 1) * len(L1_NEXT)
    J_STAT2 = J_L1O + KB
    J_OUT = J_STAT2 + 1

    def l0_job(name, i, first):
        return Job(J_L0 + L0_FIRST.index(name)) if first else Job(J_L0N + L0_NEXT.index(name), i - 1, len(L0_NEXT))

    def l1_job(name, g, first, last):
        order = L1_LAST if last else L1_NEXT
        return Job(J_L1 + L1_FIRST.index(name)) if first else Job(J_L1N + order.index(name), g - 1, len(order))

    def l0_unit(name, i):
        at = 2 + L0_UNITS.index(name)
        return (at % RAW, i * (16 * len(L0_UNITS) // RAW) + 16 * (at // RAW + 1),
                i * len(L0_SPLITS) + (3 + L0_SPLITS.index(name) if name[0] != "M" else 0), i * len(L0_UNITS) + (at + 1))

    U_L1 = 2 + HEADS * len(L0_UNITS)
    N_L1 = 2 + HEADS * len(L0_SPLITS)

    def l1_unit(name, g):
        at = U_L1 + L1_UNITS.index(name)
        return (at % RAW, g * (16 * len(L1_UNITS) // RAW) + 16 * (at // RAW + 1),
                g * len(L1_UNITS) + (N_L1 + 1 + L1_UNITS.index(name)), g * len(L1_UNITS) + (at + 1))

    with ExitStack() as ctx:
        def sb(name, shape, dt=F32, stack=ctx):
            return stack.enter_context(nc.sbuf_tensor(name, shape, dt))

        def sem(name):
            return ctx.enter_context(nc.semaphore(name))

        xT = sb("xT", [P, KB, S])
        h_hi = sb("h_hi", [P, KB, S], F32R)
        h_lo = sb("h_lo", [P, KB, S], F32R)
        w_hi = sb("w_hi", [P, 2, 1024], F32R)
        w_lo = sb("w_lo", [P, 2, 1024], F32R)
        wo_hi = sb("wo_hi", [P, 2, D], F32R)
        wo_lo = sb("wo_lo", [P, 2, D], F32R)
        g_hi = sb("g_hi", [P, 2 * P], F32R)
        g_lo = sb("g_lo", [P, 2 * P], F32R)
        y_hi = sb("y_hi", [P, 2, S], F32R)
        y_lo = sb("y_lo", [P, 2, S], F32R)
        raw = sb("raw", [P, RAW, 1024])
        mod_acc = sb("mod_acc", [P, NMOD])
        vec = sb("vec", [P, NCOL])
        rows_a = sb("rows_a", [P, P])
        rows_b = sb("rows_b", [NCOL - P, P])
        rows_c = sb("rows_c", [KB, P])
        c_col = sb("c_col", [P, KB])
        ident = sb("ident", [P, P])
        ones = sb("ones", [P, P])
        modv = sb("modv", [P, 2, 3 * KB])
        gsc = sb("gsc", [P, 2, KB])
        ca = sb("ca", [P, KB])
        sps = sb("sps", [P, 8, HEADS])
        c8 = sb("c8", [P, 2, HEADS])
        spare = sb("spare", [P, 1])
        cst = sb("cst", [P, 2])
        ss = sb("ss", [P, SB])
        sd = sb("sd", [P, 3, SB])
        rstd = sb("rstd", [P, 3, SB])
        pos = sb("pos", [P, PAD], mybir.dt.int32)
        icnt = sb("icnt", [P, GROUPS, PAD])
        fix = sb("fix", [P, PAD])

        with ExitStack() as phase:
            st0 = sb("st0", [P, 13, S], F32, phase)
        with ExitStack() as phase:
            xc_hi = sb("xc_hi", [P, S], F32R, phase)
            xc_lo = sb("xc_lo", [P, S], F32R, phase)
            scr = sb("scr", [P, 11, S], F32, phase)
        with ExitStack() as phase:
            d_hi = sb("d_hi", [P, GB, S], F32R, phase)
            d_lo = sb("d_lo", [P, GB, S], F32R, phase)
            sg = sb("sg", [P, 2, S], F32, phase)
            vp = sb("vp", [P, PAD + S], F32, phase)
            win = [sb(f"win{n}", [P, PAD + S], F32, phase) for n in range(2)]
        with ExitStack() as phase:
            ob = sb("ob", [P, SB, D], F32, phase)
        XC, GCS, Z, SC, R, G, TH, A, A2, SGA, SGB = (scr[:, n, :] for n in range(11))
        bc_sb = st0[:, SB + 4, :]
        diag0 = mod_acc[:, 2 * D:3 * D]
        x_rows, stage, gate_acc = st0[:, 0:SB, :], st0[:, SB:SB + 4, :], st0[:, SB + 4, :]
        psum = ctx.enter_context(nc.psum_tensor("psum", [P, SLOTS, 1024], F32))

        rows_in = sem("rows_in")
        c_in = sem("c_in")
        x_in = [sem(f"x_in{b}") for b in range(SB)]
        stage_in = [sem(f"stage_in{n}") for n in range(4)]
        raw_in = [sem(f"raw_in{n}") for n in range(RAW)]
        gate_x_in = sem("gate_x_in")
        out_done = sem("out_done")
        const_step = sem("const_step")
        psum_full = sem("psum_full")
        evacuated = [sem(f"evacuated{n}") for n in range(SLOTS)]
        hi_done = sem("hi_done")
        unit_done = sem("unit_done")
        small = sem("small")
        ca_sig = sem("ca_sig")
        lam_exp = sem("lam_exp")
        softplus_ready = sem("softplus_ready")
        stage_used = sem("stage_used")
        stage_summed = sem("stage_summed")
        mod_zero = sem("mod_zero")
        root_loaded = sem("root_loaded")
        ss_ready = sem("ss_ready")
        rstd_ready = sem("rstd_ready")
        xg_ready = sem("xg_ready")
        sq_ready = sem("sq_ready")
        x_half = sem("x_half")
        sq_half = sem("sq_half")
        last_sum = sem("last_sum")
        bc_half = sem("bc_half")
        xn_half = sem("xn_half")
        ssq_added = sem("ssq_added")
        sd_ready = sem("sd_ready")
        diag0_ready = sem("diag0_ready")
        diag_ready = sem("diag_ready")
        xn_ready = sem("xn_ready")
        hx_ready = sem("hx_ready")
        hhi_ready = sem("hhi_ready")
        h_first = sem("h_first")
        h_ready = sem("h_ready")
        modv_ready = sem("modv_ready")
        conv0 = sem("conv0")
        conv_tap = sem("conv_tap")
        xc_hi_ready = sem("xc_hi_ready")
        xc_ready = sem("xc_ready")
        sc0 = sem("sc0")
        sc_tap = sem("sc_tap")
        gx_done = sem("gx_done")
        th_ready = sem("th_ready")
        a_ready = sem("a_ready")
        a2_ready = sem("a2_ready")
        m2_done = sem("m2_done")
        m_ready = sem("m_ready")
        m_reset = sem("m_reset")
        u_done = sem("u_done")
        scan_done = sem("scan_done")
        sga_ready = sem("sga_ready")
        sgb_ready = sem("sgb_ready")
        y_ready = sem("y_ready")
        yhi_ready = sem("yhi_ready")
        ylo_ready = sem("ylo_ready")
        win_step = sem("win_step")
        d_ready = sem("d_ready")
        dhi_ready = sem("dhi_ready")
        dlo_ready = sem("dlo_ready")
        sg_ready = sem("sg_ready")
        pads = sem("pads")

        def pair_operands(last):
            return (w_hi, w_lo, h_hi, h_lo) if last else (wo_hi, wo_lo, y_hi, y_lo)

        def v(name, n=0, count=1):
            return vec[:, bass.ds(COL[name] + n, count)]

        DIRECT = 5

        def stage_done(unit):
            if unit == DIRECT:
                return stage_summed, 1
            return stage_used, unit + 2 if unit < DIRECT else unit + 1

        block = ctx.enter_context(nc.Block())

        @block.sync
        def _(sp):
            sp.dma_start(rows_c[:, :], c.rearrange("a (r q) -> (a r) q", q=P)).then_inc(c_in, 16)
            params = (("norm_g", norm_g), ("mod_b", mod_b), ("conv_w", hy_conv_w), ("conv_b", hy_conv_b),
                      ("b_a", lru_b_a), ("b_x", lru_b_x), ("lam", lru_lambda), ("sc_w", sc_conv_w),
                      ("pool_b", pool_b_grp), ("pool_scale", pool_scale), ("final_g", final_g))

            def parameter_rows(name, src):
                n = dict(ROWS_A + ROWS_B)[name]
                dst = rows_a[COL[name]:COL[name] + n, :] if COL[name] < P else rows_b[COL[name] - P:COL[name] - P + n, :]
                outer = " ".join("abc"[:len(src.shape) - 1])
                sp.dma_start(dst, src.rearrange(f"{outer} (r q) -> ({outer} r) q", q=P)).then_inc(rows_in, 16)

            for b in range(SB):
                sp.dma_start(x_rows[:, b, :], x[0, b * P:(b + 1) * P, :]).then_inc(x_in[b], 16)
                if b:
                    parameter_rows(*params[b - 1])

            def stage_load(unit):
                part, k = unit // KB, unit % KB
                if unit >= 4:
                    sp.wait_ge(*stage_done(unit - 4))
                rows = mod_w[0][k * P:(k + 1) * P, :]
                if part < 2:
                    src = rows[:, 0:2 * D].rearrange("p (c n) -> p c n", c=2)[:, :, part * HALF:(part + 1) * HALF]
                else:
                    src = rows[:, 2 * D:3 * D].rearrange("p (c n) -> p c n", c=2)
                sp.dma_start(stage[:, unit % 4, :].rearrange("p (c n) -> p c n", c=2), src)\
                  .then_inc(stage_in[unit % 4], 16)

            def raw_load(at, src, blocks):
                sp.dma_start(raw[:, at, :].rearrange("p (k n) -> p k n", k=blocks), src).then_inc(raw_in[at], 16)

            hy_in = hy_w_in[0].rearrange("(k p) n -> p k n", p=P)
            pool_in = pool_w_in[0].rearrange("(k p) n -> p k n", p=P)

            def l0_loads(i, last, names=L0_UNITS):
                for name in names:
                    at, _, _, done = l0_unit(name, i)
                    sp.wait_ge(unit_done, done - RAW)
                    if name == "G":
                        sp.dma_start(raw[:, at, 0:P], lru_w_a[0][i]).then_inc(raw_in[at], 16)
                        sp.dma_start(raw[:, at, P:2 * P], lru_w_x[0][i]).then_inc(gate_x_in, 16)
                    elif name[0] == "M":
                        chunk = int(name[1])
                        raw_load(at, mod_w[1][bass.ds(i * P, P), chunk * D:(chunk + 1) * D]
                                 .rearrange("p (k n) -> p k n", k=1), 1)
                    elif name in ("WoA", "WoB"):
                        raw_load(at, hy_w_out[0][bass.ds(i * P + (D if name == "WoB" else 0), P), :]
                                 .rearrange("p (k n) -> p k n", k=1), 1)
                    elif name[-1] != "'":
                        raw_load(at, hy_in[:, :, bass.ds(i * P + L0_COLS[name] * D, P)], KB)
                    elif not last:
                        raw_load(at, hy_in[:, :, bass.ds((i + 1) * P + L0_COLS[name[:-1]] * D, P)], KB)
                    else:
                        n = ("xa'", "gc'").index(name)
                        raw_load(at, pool_in[:, :, n * P:(n + 1) * P], KB)

            for unit in range(KB):
                stage_load(unit)
                if unit < len(params) - (SB - 1):
                    parameter_rows(*params[SB - 1 + unit])
                if unit == 3:
                    raw_load(0, hy_in[:, :, L0_COLS["xa"] * D:L0_COLS["xa"] * D + P], KB)
                if unit == KB - 1:
                    raw_load(1, hy_in[:, :, L0_COLS["gc"] * D:L0_COLS["gc"] * D + P], KB)
            for unit in range(KB, 2 * KB):
                stage_load(unit)
            l0_loads(0, False, L0_UNITS[:2])
            for unit in range(2 * KB, 3 * KB):
                stage_load(unit)
            l0_loads(0, False, L0_UNITS[2:])
            with sp.Fori(1, HEADS - 1) as i:
                l0_loads(i, False)
            l0_loads(HEADS - 1, True)

            def l1_loads(g, last):
                for name in L1_UNITS:
                    if last and name[-1] == "'":
                        continue
                    at, _, _, done = l1_unit(name, g)
                    sp.wait_ge(unit_done, done - RAW)
                    if name[0] == "V":
                        turn = (g + 1) if name[-1] == "'" else g
                        raw_load(at, pool_in[:, :, bass.ds(turn * (GB * P) + int(name[1]) * P, P)], KB)
                    elif name[0] == "G":
                        raw_load(at, pool_in[:, :, bass.ds(g * (GB * P) + (2 * D + int(name[1]) * P), P)], KB)
                    elif name[0] == "M":
                        n = int(name[1]) * P
                        raw_load(at, pool_w_grp[0][g].rearrange("(k p) n -> p k n", p=P)[:, :, n:n + 2 * P], GB)
                    else:
                        raw_load(at, pool_w_out[0][bass.ds(g * (GB * P) + "ABCD".index(name[2]) * P, P), :]
                                 .rearrange("p (k n) -> p k n", k=1), 1)

            with sp.Fori(0, GROUPS - 1) as g:
                l1_loads(g, False)
            l1_loads(GROUPS - 1, True)

            for b in range(SB):
                j = Job(J_OUT + b)
                sp.wait_ge(evacuated[j.slot], j.read)
                sp.dma_start(out[0, b * P:(b + 1) * P, :], ob[:, b, :]).then_inc(out_done, 16)
            sp.wait_ge(out_done, 16 * SB)

        HALVES = [slice(hh * HALF, (hh + 1) * HALF) for hh in range(NH)]

        def h_count(turn, k, hh=NH - 1):
            return turn * KB + k + 1 + sum(first < (turn, k) for first in FIRST_H) + (hh if (turn, k) in FIRST_H else 0)

        FIRST_H = {(0, 0): diag0, (0, KB // 2): x_rows[:, 0, :], (1, 0): scr[:, 8, :]}
        LAM_STEPS = 3
        CONSTS = 6

        @block.gpsimd
        def _(pool):
            nc.gpsimd.memset(ident[:, :], 0.0).then_inc(const_step, 1)
            nc.gpsimd.memset(ones[:, :], 1.0).then_inc(const_step, 1)
            nc.gpsimd.memset(cst[:, 0:1], EPS).then_inc(const_step, 1)
            nc.gpsimd.memset(cst[:, 1:2], TINY).then_inc(const_step, 1)
            nc.gpsimd.iota(pos[:, :], [[1, PAD]], base=1, channel_multiplier=0).then_inc(const_step, 1)
            pool.wait_ge(const_step, 5)
            nc.gpsimd.affine_select(out=ident[:, :], in_=ident[:, :], compare_op=ALU.not_equal, fill=1.0, base=0,
                                    pattern=[[-1, P]], channel_multiplier=1).then_inc(const_step, 1)
            nc.gpsimd.memset(mod_acc[:, 0:2 * D], 0.0).then_inc(stage_used, 1)
            pool.wait_ge(rstd_ready, 1)
            for b in range(SB):
                nc.gpsimd.tensor_scalar(diag0[:, b * P:(b + 1) * P], ident[:, :], rstd[:, 0, b:b + 1], None, ALU.mult)\
                  .then_inc(diag0_ready, 1)
            pool.wait_ge(evacuated[Job(J_BC0).slot], Job(J_BC0).read)
            for k in range(KB):
                nc.gpsimd.tensor_tensor(x_rows[:, k, :], xT[:, k, :], bc_sb, ALU.mult).then_inc(xn_ready, 1)
            pool.wait_ge(psum_full, Job(J_MOD0 + 1).full)
            nc.gpsimd.memset(mod_acc[:, :], 0.0).then_inc(mod_zero, 1)

        @block.scalar
        def _(act):
            def split_hi(dst, unit, n=1024, second=None):
                slot, landed, _, _ = unit
                act.wait_ge(raw_in[slot], landed)
                if second is not None:
                    act.wait_ge(gate_x_in, second)
                nc.scalar.activation(dst, raw[:, slot, 0:n], ACT.Copy).then_inc(hi_done, 1)

            hx_count = [0]

            def load_root():
                nc.scalar.activation(spare[:, :], cst[:, 0:1], ACT.Sqrt).then_inc(root_loaded, 1)

            def squares(k, turn, sq):
                if k >= 2:
                    act.wait_ge(ssq_added, (turn - 1) * (KB - 2) + k - 1)
                nc.scalar.activation(sq[k % 2], xT[:, k, :], ACT.Square).then_inc(sq_ready, 1)

            def last_square(turn, job, sq):
                act.wait_ge(ssq_added, turn * (KB - 2))
                for cols, written, value, done in ((HALVES[0], x_half, turn, sq_half),
                                                   (HALVES[1], evacuated[job.slot], job.read, sq_ready)):
                    act.wait_ge(written, value)
                    nc.scalar.activation(sq[1][:, cols], xT[:, KB - 1, cols], ACT.Square).then_inc(done, 1)

            def root(turn, job):
                act.wait_ge(psum_full, job.full)
                nc.scalar.activation(sd[:, turn, :], psum[:, job.slot, 0:SB], ACT.Sqrt, scale=1.0 / D,
                                     bias=cst[:, 0:1]).then_inc(sd_ready, 1)

            def modulate(turn, hx):
                for k in range(KB):
                    if turn == 0 and k % (KB // 2) == 0:
                        act.wait_ge(modv_ready, 2 * k // KB + 1)
                    if (turn, k) in FIRST_H:
                        for hh, cols in enumerate(HALVES):
                            if turn and hh == 0:
                                act.wait_ge(xn_half, 1)
                            else:
                                act.wait_ge(xn_ready, turn * KB + k + 1)
                            nc.scalar.activation(h_hi[:, k, cols], hx[k % len(hx)][:, cols], ACT.Identity,
                                                 scale=gsc[:, turn, k:k + 1], bias=modv[:, turn, k:k + 1])\
                              .then_inc(hhi_ready, 1)
                        continue
                    if turn and k == KB - 1:
                        act.wait_ge(evacuated[Job(J_BC1).slot], Job(J_BC1).read)
                    else:
                        act.wait_ge(xn_ready, turn * KB + k + 1)
                    hx_count[0] += 1
                    nc.scalar.activation(hx[k % len(hx)], hx[k % len(hx)], ACT.Identity, scale=gsc[:, turn, k:k + 1],
                                         bias=modv[:, turn, k:k + 1]).then_inc(hx_ready, 1)
                    act.wait_ge(hx_ready, hx_count[0])
                    nc.scalar.activation(h_hi[:, k, :], hx[k % len(hx)], ACT.Copy).then_inc(hhi_ready, 1)

            act.wait_ge(evacuated[Job(J_C).slot], Job(J_C).read)
            nc.scalar.activation(ca[:, :], c_col[:, :], ACT.Sigmoid).then_inc(ca_sig, 1)
            act.wait_ge(const_step, CONSTS)
            load_root()
            for b in range(SB):
                act.wait_ge(x_in[b], 16)
                if b >= 2:
                    act.wait_ge(ss_ready, b - 1)
                nc.scalar.activation(y_hi[:, b % 2, :], x_rows[:, b, :], ACT.Square, accum_out=ss[:, b:b + 1])\
                  .then_inc(ss_ready, 1)
            act.wait_ge(ss_ready, SB)
            nc.scalar.activation(sd[:, 0, :], ss[:, :], ACT.Sqrt, scale=1.0 / D, bias=cst[:, 0:1]).then_inc(sd_ready, 1)
            split_hi(w_hi[:, 0, :], (0, 16, None, None))
            act.wait_ge(small, LAM_STEPS)
            nc.scalar.activation(sps[:, 1, :], sps[:, 0, :], ACT.Exp).then_inc(lam_exp, 1)
            j = Job(J_BC0)
            act.wait_ge(psum_full, j.full)
            for b in range(SB - SLOTS, SB):
                act.wait_ge(evacuated[Job(J_XT + b).slot], Job(J_XT + b).read)
            nc.scalar.activation(bc_sb, psum[:, j.slot, :], ACT.Copy).then_inc(evacuated[j.slot], 1)
            split_hi(w_hi[:, 1, :], (1, 16, None, None))
            modulate(0, [x_rows[:, k, :] for k in range(KB)])

            def l0(i, first):
                def job(name):
                    return l0_job(name, i, first)

                def output_rows(m):
                    split_hi(wo_hi[:, m, :], l0_unit(("WoA", "WoB")[m], i))

                act.wait_ge(psum_full, job("xa").full)
                split_hi(w_hi[:, 0, :], l0_unit("v", i))
                if not first:
                    act.wait_ge(gx_done, i)
                nc.scalar.activation(XC, psum[:, job("xa").slot, :], ACT.Identity, scale=v("conv_w", 3 * HEADS + i),
                                     bias=v("conv_b", i)).then_inc(conv0, 1)
                split_hi(g_hi[:, :], l0_unit("G", i), 2 * P, 16 * (i + 1))
                act.wait_ge(evacuated[job("xa").slot], job("xa").read)
                nc.scalar.activation(xc_hi[:, :], XC, ACT.Copy).then_inc(xc_hi_ready, 1)
                act.wait_ge(psum_full, job("gc").full)
                split_hi(w_hi[:, 1, :], l0_unit("ga", i))
                nc.scalar.activation(GCS, psum[:, job("gc").slot, :], ACT.Copy).then_inc(evacuated[job("gc").slot], 1)
                act.wait_ge(psum_full, job("v").full)
                split_hi(w_hi[:, 0, :], l0_unit("gbp", i))
                act.wait_ge(evacuated[job("v").slot], job("v").read)
                if not first:
                    act.wait_ge(y_ready, 2 * i)
                nc.scalar.activation(SC, Z, ACT.Copy, scale=v("sc_w", 2 * HEADS + i)).then_inc(sc0, 1)
                act.wait_ge(psum_full, job("r").full)
                nc.scalar.activation(R, psum[:, job("r").slot, :], ACT.Sigmoid, bias=v("b_a", i))\
                  .then_inc(evacuated[job("r").slot], 1)
                act.wait_ge(psum_full, job("i").full)
                nc.scalar.activation(G, psum[:, job("i").slot, :], ACT.Sigmoid, bias=v("b_x", i))\
                  .then_inc(evacuated[job("i").slot], 1)
                act.wait_ge(evacuated[job("r").slot], job("r").read)
                if first:
                    output_rows(0)
                    act.wait_ge(softplus_ready, 1)
                nc.scalar.activation(TH, R, ACT.Tanh, scale=c8[:, 0, bass.ds(i, 1)]).then_inc(th_ready, 1)
                nc.scalar.activation(A, R, ACT.Exp, scale=c8[:, 1, bass.ds(i, 1)]).then_inc(a_ready, 1)
                act.wait_ge(a_ready, i + 1)
                nc.scalar.activation(A2, A, ACT.Square).then_inc(a2_ready, 1)
                if first:
                    output_rows(1)
                act.wait_ge(m2_done, i + 1)
                nc.scalar.activation(A2, TH, ACT.Sqrt, bias=cst[:, 1:2]).then_inc(m_ready, 1)
                if not first:
                    act.wait_ge(psum_full, job("O7").full)
                    output_rows(0)
                    output_rows(1)
                act.wait_ge(psum_full, job("ga").full)
                split_hi(w_hi[:, 1, :], l0_unit("gb", i))
                nc.scalar.activation(SGA, psum[:, job("ga").slot, :], ACT.Sigmoid).then_inc(sga_ready, 1)
                act.wait_ge(psum_full, job("gbp").full)
                split_hi(w_hi[:, 0, :], l0_unit("xa'", i))
                act.wait_ge(y_ready, 2 * i + 1)
                nc.scalar.activation(y_hi[:, 0, :], SGA, ACT.Copy).then_inc(yhi_ready, 1)
                act.wait_ge(psum_full, job("gb").full)
                nc.scalar.activation(SGB, psum[:, job("gb").slot, :], ACT.Sigmoid).then_inc(sgb_ready, 1)
                split_hi(w_hi[:, 1, :], l0_unit("gc'", i))
                act.wait_ge(y_ready, 2 * i + 2)
                nc.scalar.activation(y_hi[:, 1, :], SGB, ACT.Copy).then_inc(yhi_ready, 1)

            l0(0, True)
            with act.Fori(1, HEADS) as i:
                l0(i, False)

            act.wait_ge(root_loaded, 1)
            load_root()
            sq = (scr[:, 0, :], scr[:, 1, :])
            for k in range(KB - 1):
                act.wait_ge(evacuated[Job(J_L0O + k).slot], Job(J_L0O + k).read)
                squares(k, 1, sq)
            last_square(1, Job(J_L0O + KB - 1), sq)
            root(1, Job(J_STAT1))
            act.wait_ge(modv_ready, 3)
            modulate(1, [scr[:, 4 + n, :] for n in range(4)])

            def l1(g, first, last):
                def job(name):
                    return l1_job(name, g, first, last)

                def unit(name):
                    return l1_unit(name, g)

                def pair_y(n):
                    for m in range(2):
                        j = job(f"M{n + m}")
                        act.wait_ge(evacuated[j.slot], j.read)
                        nc.scalar.activation((y_hi if n == 0 else pair_operands(last)[2])[:, m, :], sg[:, m, :],
                                             ACT.Copy).then_inc(yhi_ready, 1)

                def gates(n):
                    j = job(f"G{n}")
                    act.wait_ge(ylo_ready, GB * g + (2 * HEADS + n - 1))
                    nc.scalar.activation(sg[:, n % 2, :], psum[:, j.slot, :], ACT.Sigmoid).then_inc(sg_ready, 1)

                for n in range(GB):
                    j = job(f"V{n}")
                    act.wait_ge(psum_full, j.full)
                    split_hi(w_hi[:, n % 2, :], unit(("V2", "V3", "G0", "G1")[n]))
                    if n or not first:
                        act.wait_ge(dlo_ready, GB * g + n)
                    nc.scalar.activation(vp[:, PAD:], psum[:, j.slot, :], ACT.Copy).then_inc(evacuated[j.slot], 1)
                    act.wait_ge(d_ready, GB * g + (n + 1))
                    nc.scalar.activation(d_hi[:, n, :], vp[:, PAD:], ACT.Copy).then_inc(dhi_ready, 1)
                if not first:
                    act.wait_ge(psum_full, job("Q7").full)
                split_hi(wo_hi[:, 0, :], unit("WoA"))
                split_hi(wo_hi[:, 1, :], unit("WoB"))
                act.wait_ge(psum_full, job("G0").full)
                split_hi(w_hi[:, 0, :], unit("M01"))
                gates(0)
                act.wait_ge(psum_full, job("G1").full)
                split_hi(w_hi[:, 1, :], unit("G2"))
                gates(1)
                act.wait_ge(psum_full, job("M1").full)
                split_hi(w_hi[:, 0, :], unit("G3"))
                pair_y(0)
                act.wait_ge(psum_full, job("G2").full)
                split_hi(w_hi[:, 1, :], unit("M23"))
                gates(2)
                act.wait_ge(psum_full, job("G3").full)
                gates(3)
                if last:
                    split_hi(w_hi[:, 0, :], unit("WoC"))
                    act.wait_ge(psum_full, job("M3").full)
                    split_hi(w_hi[:, 1, :], unit("WoD"))
                else:
                    act.wait_ge(psum_full, job("O7").full)
                    split_hi(wo_hi[:, 0, :], unit("WoC"))
                    split_hi(wo_hi[:, 1, :], unit("WoD"))
                    split_hi(w_hi[:, 0, :], unit("V0'"))
                    act.wait_ge(psum_full, job("M3").full)
                    split_hi(w_hi[:, 1, :], unit("V1'"))
                pair_y(2)

            l1(0, True, False)
            with act.Fori(1, GROUPS - 1) as g:
                l1(g, False, False)
            l1(GROUPS - 1, False, True)

            act.wait_ge(root_loaded, 2)
            load_root()
            sq = (sg[:, 0, :], sg[:, 1, :])
            act.wait_ge(ylo_ready, 2 * HEADS + GB * GROUPS)
            for k in range(KB):
                if k < KB - 1:
                    act.wait_ge(evacuated[Job(J_L1O + k).slot], Job(J_L1O + k).read)
                    squares(k, 2, sq)
                else:
                    last_square(2, Job(J_L1O + k), sq)
                    act.wait_ge(sq_half, 2)
                    act.wait_ge(sq_ready, 2 * KB)
                nc.scalar.activation(xT[:, k, :], xT[:, k, :], ACT.Copy, scale=v("final_g", k)).then_inc(xg_ready, 1)
            root(2, Job(J_STAT2))
            act.wait_ge(evacuated[Job(J_STAT2).slot], Job(J_STAT2).read)
            for b in range(0, SB, 2):
                j = Job(J_OUT + b)
                act.wait_ge(psum_full, j.full)
                nc.scalar.activation(ob[:, b, :], psum[:, j.slot, :], ACT.Copy, scale=rstd[:, 2, b:b + 1])\
                  .then_inc(evacuated[j.slot], 1)

        @block.vector
        def _(dve):
            smalls = [0]

            def step(ins):
                smalls[0] += 1
                ins.then_inc(small, 1)
                dve.wait_ge(small, smalls[0])

            def split_lo(dst, hi, unit, n=1024):
                slot, _, done, _ = unit
                dve.wait_ge(hi_done, done)
                nc.vector.tensor_tensor(dst, raw[:, slot, 0:n], hi.bitcast(F32), ALU.subtract).then_inc(unit_done, 1)

            dve.wait_ge(psum_full, Job(J_C).full)
            nc.vector.tensor_copy(c_col[:, :], psum[:, J_C, 0:KB]).then_inc(evacuated[J_C], 1)
            for b in range(SB):
                j = Job(J_XT + b)
                dve.wait_ge(psum_full, j.full)
                nc.vector.tensor_copy(xT[:, :, b * P:(b + 1) * P], psum[:, j.slot, :].rearrange("p (k n) -> p k n", k=KB))\
                  .then_inc(evacuated[j.slot], 1)
                if b == 0:
                    dve.wait_ge(ca_sig, 1)
                    step(nc.vector.tensor_tensor(ca[:, :], ca[:, :], c_col[:, :], ALU.mult))

            def add_unit(dst, src, k, signal):
                nc.vector.scalar_tensor_tensor(out=dst, in0=src, scalar=ca[:, bass.ds(k, 1)], in1=dst, op0=ALU.mult,
                                               op1=ALU.add).then_inc(signal, 1)

            def modulation(layer, blocks, job):
                lo, hi = blocks
                dve.wait_ge(psum_full, job.full)
                at = COL["mod_b"] + layer * 3 * KB
                nc.vector.tensor_tensor(modv[:, layer, lo:hi], psum[:, job.slot, 0:hi - lo],
                                        vec[:, at + lo:at + hi], ALU.add).then_inc(evacuated[job.slot], 1)

            def scale_norm(layer, job):
                dve.wait_ge(evacuated[job.slot], job.read)
                nc.vector.scalar_tensor_tensor(out=gsc[:, layer, :], in0=modv[:, layer, KB:2 * KB], scalar=1.0,
                                               in1=vec[:, COL["norm_g"] + layer * KB:COL["norm_g"] + (layer + 1) * KB],
                                               op0=ALU.add, op1=ALU.mult).then_inc(modv_ready, 1)

            def sum_squares(k, turn, sq, ssq):
                dve.wait_ge(sq_ready, (turn - 1) * KB + k + 1)
                if k == 0:
                    ins = nc.vector.tensor_copy(ssq, sq[0])
                else:
                    dve.wait_ge(ssq_added, (turn - 1) * (KB - 2) + k)
                    ins = nc.vector.tensor_tensor(ssq, ssq, sq[k % 2], ALU.add)
                ins.then_inc(ssq_added, 1)

            def last_block(turn, job, sq):
                for cols, done in ((HALVES[0], x_half), (HALVES[1], evacuated[job.slot])):
                    if done is x_half:
                        dve.wait_ge(psum_full, job.full)
                    nc.vector.scalar_tensor_tensor(out=xT[:, KB - 1, cols], in0=psum[:, job.slot, cols],
                                                   scalar=modv[:, turn - 1, 3 * KB - 1:3 * KB], in1=xT[:, KB - 1, cols],
                                                   op0=ALU.mult, op1=ALU.add).then_inc(done, 1)
                for cols, ready, value in ((HALVES[0], sq_half, turn), (HALVES[1], sq_ready, turn * KB)):
                    dve.wait_ge(ready, value)
                    nc.vector.tensor_tensor(sq[0][:, cols], sq[0][:, cols], sq[1][:, cols], ALU.add)\
                      .then_inc(last_sum, 1)

            def inverse(turn, job):
                dve.wait_ge(sd_ready, turn + 1)
                done, value = (evacuated[job.slot], job.read) if job else (rstd_ready, 1)
                nc.vector.reciprocal(rstd[:, turn, :], sd[:, turn, :]).then_inc(done, 1)
                dve.wait_ge(done, value)

            def diagonals(turn, diag):
                for b in range(SB):
                    nc.vector.tensor_scalar(diag[:, b * P:(b + 1) * P], ident[:, :], rstd[:, turn, b:b + 1], None,
                                            ALU.mult).then_inc(diag_ready, 1)

            def h_low(k, turn, hx):
                if (turn, k) in FIRST_H:
                    place, at = FIRST_H[turn, k], list(FIRST_H).index((turn, k))
                    dve.wait_ge(modv_ready, at + 1)
                    for hh, cols in enumerate(HALVES):
                        if turn:
                            normalize_first(hh, hx)
                        nc.vector.tensor_scalar(place[:, cols], hx[k % len(hx)][:, cols], gsc[:, turn, k:k + 1],
                                                modv[:, turn, k:k + 1], ALU.mult, ALU.add).then_inc(h_first, 1)
                    for hh, cols in enumerate(HALVES):
                        dve.wait_ge(h_first, NH * at + hh + 1)
                        dve.wait_ge(hhi_ready, h_count(turn, k, hh))
                        nc.vector.tensor_tensor(h_lo[:, k, cols], place[:, cols], h_hi[:, k, cols].bitcast(F32),
                                                ALU.subtract).then_inc(h_ready, 1)
                    return
                dve.wait_ge(hhi_ready, h_count(turn, k))
                nc.vector.tensor_tensor(h_lo[:, k, :], hx[k % len(hx)], h_hi[:, k, :].bitcast(F32), ALU.subtract)\
                  .then_inc(h_ready, 1)

            def normalize_first(hh, hx):
                ready, value = (bc_half, 2) if hh == 0 else (psum_full, Job(J_BC1).full)
                dve.wait_ge(ready, value)
                done, value = (xn_half, 1) if hh == 0 else (xn_ready, KB + 1)
                nc.vector.tensor_tensor(hx[0][:, HALVES[hh]], xT[:, 0, HALVES[hh]], psum[:, Job(J_BC1).slot, HALVES[hh]],
                                        ALU.mult).then_inc(done, 1)
                dve.wait_ge(done, value)

            def normalize(turn, job, hx):
                h_low(0, turn, hx)
                for k in range(1, KB + 2):
                    if k < KB:
                        if k >= 4:
                            dve.wait_ge(h_ready, h_count(turn, k - 4))
                        nc.vector.tensor_tensor(hx[k % 4], xT[:, k, :], psum[:, job.slot, :], ALU.mult)\
                          .then_inc(xn_ready if k < KB - 1 else evacuated[job.slot], 1)
                    if k >= 3:
                        h_low(k - 2, turn, hx)

            def softplus():
                e, ratio, square, series, result = (sps[:, n, :] for n in (1, 2, 3, 4, 5))
                terms = 9
                dve.wait_ge(lam_exp, 1)
                step(nc.vector.tensor_scalar(series, e, 2.0, None, ALU.add))
                step(nc.vector.reciprocal(ratio, series))
                step(nc.vector.tensor_tensor(ratio, ratio, e, ALU.mult))
                step(nc.vector.tensor_tensor(square, ratio, ratio, ALU.mult))
                step(nc.vector.tensor_scalar(series, square, 1.0 / (2 * terms + 1), None, ALU.mult))
                for n in range(terms - 1, 0, -1):
                    step(nc.vector.scalar_tensor_tensor(out=series, in0=series, scalar=1.0 / (2 * n + 1), in1=square,
                                                        op0=ALU.add, op1=ALU.mult))
                step(nc.vector.scalar_tensor_tensor(out=series, in0=series, scalar=1.0, in1=ratio, op0=ALU.add,
                                                    op1=ALU.mult))
                step(nc.vector.tensor_scalar(result, v("lam", 0, HEADS), -1.0, 0.0, ALU.mult, ALU.max))
                step(nc.vector.scalar_tensor_tensor(out=result, in0=series, scalar=2.0, in1=result, op0=ALU.mult,
                                                    op1=ALU.add))
                step(nc.vector.tensor_scalar(c8[:, 0, :], result, LRU_C, None, ALU.mult))
                nc.vector.tensor_scalar(c8[:, 1, :], result, -LRU_C, None, ALU.mult).then_inc(softplus_ready, 1)

            def stage_add(unit):
                part, k = unit // KB, unit % KB
                dve.wait_ge(stage_in[unit % 4], 16 * (unit // 4 + 1))
                if unit == 2 * KB:
                    dve.wait_ge(xn_ready, KB)
                    nc.vector.tensor_scalar(gate_acc, stage[:, 0, :], ca[:, 0:1], None, ALU.mult).then_inc(stage_used, 1)
                    return
                dve.wait_ge(stage_used, stage_done(unit)[1] - 1)
                add_unit(mod_acc[:, part * D:(part + 1) * D] if part < 2 else gate_acc, stage[:, unit % 4, :], k,
                         stage_used)

            def modulation_half(half):
                job, blocks = Job(J_MOD0 + half), slice(half * KB // 2, (half + 1) * KB // 2)
                dve.wait_ge(psum_full, job.full)
                nc.vector.tensor_tensor(modv[:, 0, 0:2 * KB].rearrange("p (c k) -> p c k", c=2)[:, :, blocks],
                                        psum[:, job.slot, 0:KB].rearrange("p (c k) -> p c k", c=2),
                                        v("mod_b", 0, 2 * KB).rearrange("p (c k) -> p c k", c=2)[:, :, blocks], ALU.add)\
                  .then_inc(evacuated[job.slot], 1)
                dve.wait_ge(evacuated[job.slot], job.read)
                nc.vector.scalar_tensor_tensor(out=gsc[:, 0, blocks], in0=modv[:, 0, KB:2 * KB][:, blocks], scalar=1.0,
                                               in1=v("norm_g", 0, KB)[:, blocks], op0=ALU.add, op1=ALU.mult)\
                  .then_inc(modv_ready, 1)

            hx0 = [x_rows[:, k, :] for k in range(KB)]
            inverse(0, None)
            for k in range(4):
                stage_add(k)
            j = Job(J_VEC)
            dve.wait_ge(psum_full, j.full)
            nc.vector.tensor_copy(vec[:, :], psum[:, j.slot, 0:NCOL]).then_inc(evacuated[j.slot], 1)
            dve.wait_ge(evacuated[j.slot], j.read)
            step(nc.vector.tensor_scalar(sps[:, 0, :], v("lam", 0, HEADS), -1.0, None, ALU.mult))
            step(nc.vector.tensor_tensor(sps[:, 0, :], sps[:, 0, :], v("lam", 0, HEADS), ALU.min))
            assert smalls[0] == LAM_STEPS
            stage_add(4)
            split_lo(w_lo[:, 0, :], w_hi[:, 0, :], (0, None, 1, None))
            stage_add(6)
            stage_add(7)
            split_lo(w_lo[:, 1, :], w_hi[:, 1, :], (1, None, 2, None))
            stage_add(KB)
            modulation_half(0)
            dve.wait_ge(xn_ready, 1)
            unit = KB + 1
            for k in range(KB // 2):
                h_low(k, 0, hx0)
                for _ in range(1 if k == KB // 2 - 2 else 2):
                    stage_add(unit)
                    unit += 1
            modulation_half(1)
            dve.wait_ge(xn_ready, KB // 2 + 1)
            for k in range(KB // 2, KB):
                h_low(k, 0, hx0)
                stage_add(2 * KB + k - KB // 2)

            def residual(k, layer, job):
                dve.wait_ge(psum_full, job.full)
                nc.vector.scalar_tensor_tensor(out=xT[:, k, :], in0=psum[:, job.slot, :],
                                               scalar=modv[:, layer, 2 * KB + k:2 * KB + k + 1], in1=xT[:, k, :],
                                               op0=ALU.mult, op1=ALU.add).then_inc(evacuated[job.slot], 1)

            def add_mod(i, chunk):
                slot, landed, _, done = l0_unit(f"M{chunk}", i)
                dve.wait_ge(raw_in[slot], landed)
                dve.wait_ge(unit_done, done - 1)
                add_unit(mod_acc[:, chunk * D:(chunk + 1) * D], raw[:, slot, :], i, unit_done)

            def l0(i, first):
                def job(name):
                    return l0_job(name, i, first)

                def outs(*blocks):
                    if not first:
                        for k in blocks:
                            residual(k, 0, job(f"O{k}"))

                def output_rows(m):
                    split_lo(wo_lo[:, m, :], wo_hi[:, m, :], l0_unit(("WoA", "WoB")[m], i))

                split_lo(w_lo[:, 0, :], w_hi[:, 0, :], l0_unit("v", i))
                xa = job("xa")
                dve.wait_ge(conv0, i + 1)
                for n, back in enumerate((1, 2, 3)):
                    if n:
                        dve.wait_ge(conv_tap, 2 * i + n)
                    nc.vector.scalar_tensor_tensor(out=XC[:, back:], in0=psum[:, xa.slot, 0:S - back],
                                                   scalar=v("conv_w", (3 - back) * HEADS + i), in1=XC[:, back:],
                                                   op0=ALU.mult, op1=ALU.add)\
                      .then_inc(conv_tap if n < 2 else evacuated[xa.slot], 1)
                split_lo(g_lo[:, :], g_hi[:, :], l0_unit("G", i), 2 * P)
                outs(0, 1)
                if first:
                    stage_add(3 * KB - 4)
                    stage_add(3 * KB - 3)
                dve.wait_ge(xc_hi_ready, i + 1)
                nc.vector.tensor_tensor(xc_lo[:, :], XC, xc_hi[:, :].bitcast(F32), ALU.subtract).then_inc(xc_ready, 1)
                split_lo(w_lo[:, 1, :], w_hi[:, 1, :], l0_unit("ga", i))
                if first:
                    stage_add(3 * KB - 2)
                    stage_add(3 * KB - 1)
                    dve.wait_ge(mod_zero, 1)
                add_mod(i, 0)
                outs(2, 3)
                gc, vj = job("gc"), job("v")
                dve.wait_ge(evacuated[gc.slot], gc.read)
                dve.wait_ge(psum_full, vj.full)
                nc.vector.tensor_tensor(Z, psum[:, vj.slot, :], GCS, ALU.mult).then_inc(evacuated[vj.slot], 1)
                split_lo(w_lo[:, 0, :], w_hi[:, 0, :], l0_unit("gbp", i))
                if first:
                    softplus()
                add_mod(i, 1)
                if first:
                    output_rows(0)
                outs(4)
                dve.wait_ge(sc0, i + 1)
                for n, back in enumerate((1, 2)):
                    if n:
                        dve.wait_ge(sc_tap, 2 * i + 1)
                    nc.vector.scalar_tensor_tensor(out=SC[:, back:], in0=Z[:, 0:S - back],
                                                   scalar=v("sc_w", (2 - back) * HEADS + i), in1=SC[:, back:],
                                                   op0=ALU.mult, op1=ALU.add).then_inc(sc_tap, 1)
                outs(5)
                if first:
                    modulation(0, (2 * KB, 3 * KB), job("GM"))
                    dve.wait_ge(evacuated[job("GM").slot], job("GM").read)
                ij = job("i")
                dve.wait_ge(evacuated[ij.slot], ij.read)
                nc.vector.tensor_tensor(G, G, XC, ALU.mult).then_inc(gx_done, 1)
                dve.wait_ge(th_ready, i + 1)
                dve.wait_ge(a2_ready, i + 1)
                nc.vector.scalar_tensor_tensor(out=TH, in0=A2, scalar=1.0, in1=TH, op0=ALU.add, op1=ALU.mult)\
                  .then_inc(m2_done, 1)
                if first:
                    output_rows(1)
                outs(6, 7)
                dve.wait_ge(m_ready, i + 1)
                nc.vector.memset(A2[:, 0:1], 1.0).then_inc(m_reset, 1)
                dve.wait_ge(m_reset, i + 1)
                dve.wait_ge(gx_done, i + 1)
                nc.vector.tensor_tensor(G, G, A2, ALU.mult).then_inc(u_done, 1)
                dve.wait_ge(u_done, i + 1)
                nc.vector.tensor_tensor_scan(R, A, G, 0.0, ALU.mult, ALU.add).then_inc(scan_done, 1)
                if not first:
                    output_rows(0)
                    output_rows(1)
                split_lo(w_lo[:, 1, :], w_hi[:, 1, :], l0_unit("gb", i))
                ga = job("ga")
                dve.wait_ge(sga_ready, i + 1)
                nc.vector.tensor_tensor(SGA, psum[:, ga.slot, :], SGA, ALU.mult).then_inc(evacuated[ga.slot], 1)
                dve.wait_ge(evacuated[ga.slot], ga.read)
                dve.wait_ge(scan_done, i + 1)
                nc.vector.tensor_tensor(SGA, SGA, R, ALU.mult).then_inc(y_ready, 1)
                add_mod(i, 2)
                split_lo(w_lo[:, 0, :], w_hi[:, 0, :], l0_unit("xa'", i))
                gbp = job("gbp")
                dve.wait_ge(psum_full, gbp.full)
                dve.wait_ge(sc_tap, 2 * i + 2)
                nc.vector.tensor_tensor(SC, psum[:, gbp.slot, :], SC, ALU.mult).then_inc(evacuated[gbp.slot], 1)
                dve.wait_ge(yhi_ready, 2 * i + 1)
                nc.vector.tensor_tensor(y_lo[:, 0, :], SGA, y_hi[:, 0, :].bitcast(F32), ALU.subtract)\
                  .then_inc(ylo_ready, 1)
                gb = job("gb")
                dve.wait_ge(sgb_ready, i + 1)
                nc.vector.tensor_tensor(SGB, psum[:, gb.slot, :], SGB, ALU.mult).then_inc(evacuated[gb.slot], 1)
                dve.wait_ge(evacuated[gb.slot], gb.read)
                dve.wait_ge(evacuated[gbp.slot], gbp.read)
                nc.vector.tensor_tensor(SGB, SGB, SC, ALU.mult).then_inc(y_ready, 1)
                split_lo(w_lo[:, 1, :], w_hi[:, 1, :], l0_unit("gc'", i))
                dve.wait_ge(yhi_ready, 2 * i + 2)
                nc.vector.tensor_tensor(y_lo[:, 1, :], SGB, y_hi[:, 1, :].bitcast(F32), ALU.subtract)\
                  .then_inc(ylo_ready, 1)

            l0(0, True)
            with dve.Fori(1, HEADS) as i:
                l0(i, False)

            modulation(1, (0, 2 * KB), Job(J_MOD1))
            scale_norm(1, Job(J_MOD1))
            sq, ssq = (scr[:, 0, :], scr[:, 1, :]), scr[:, 2, :]
            for k in range(KB - 1):
                residual(k, 0, Job(J_L0O + k))
                if k:
                    sum_squares(k - 1, 1, sq, ssq)
            last_block(1, Job(J_L0O + KB - 1), sq)
            inverse(1, Job(J_STAT1))
            diagonals(1, scr[:, 3, :])
            modulation(1, (2 * KB, 3 * KB), Job(J_GATE1))
            normalize(1, Job(J_BC1), [scr[:, 4 + n, :] for n in range(4)])

            step(nc.vector.tensor_copy(fix[:, :], pos[:, :]))
            for n in range(GROUPS):
                step(nc.vector.tensor_scalar(icnt[:, n, :], fix[:, :], float(WINDOWS[n]), None, ALU.min))
                step(nc.vector.reciprocal(icnt[:, n, :], icnt[:, n, :]))
            for buf in (vp, *win):
                nc.vector.memset(buf[:, 0:PAD], 0.0).then_inc(pads, 1)
            dve.wait_ge(pads, 3)

            sums = [0]

            def l1(g):
                first, last = g == 0, g == GROUPS - 1

                def job(name):
                    return l1_job(name, g, first, last)

                def unit(name):
                    return l1_unit(name, g)

                def window_step(ins):
                    sums[0] += 1
                    ins.then_inc(win_step, 1)
                    dve.wait_ge(win_step, sums[0])

                def queued(*blocks):
                    if not first:
                        for k in blocks:
                            residual(k, 1, job(f"Q{k}"))

                def outs(*blocks):
                    for k in blocks:
                        residual(k, 1, job(f"O{k}"))

                def pool_block(n):
                    vj = job(f"V{n}")
                    dve.wait_ge(evacuated[vj.slot], vj.read)
                    src, width, turn = vp, 1, 0
                    while width < WINDOWS[g]:
                        dst = win[turn % 2]
                        window_step(nc.vector.tensor_tensor(dst[:, width:], src[:, width:], src[:, 0:PAD + S - width],
                                                            ALU.add))
                        src, width, turn = dst, 2 * width, turn + 1
                    window_step(nc.vector.tensor_tensor(fix[:, :], src[:, PAD:2 * PAD], icnt[:, g, :], ALU.mult))
                    window_step(nc.vector.tensor_tensor(vp[:, PAD:2 * PAD], fix[:, :], vp[:, PAD:2 * PAD], ALU.subtract))
                    nc.vector.scalar_tensor_tensor(out=vp[:, 2 * PAD:], in0=src[:, 2 * PAD:], scalar=1.0 / WINDOWS[g],
                                                   in1=vp[:, 2 * PAD:], op0=ALU.mult, op1=ALU.subtract)\
                      .then_inc(d_ready, 1)

                def pool_lo(n):
                    dve.wait_ge(dhi_ready, GB * g + n + 1)
                    nc.vector.tensor_tensor(d_lo[:, n, :], vp[:, PAD:], d_hi[:, n, :].bitcast(F32), ALU.subtract)\
                      .then_inc(dlo_ready, 1)

                def gates(n):
                    j = job(f"G{n}")
                    dve.wait_ge(sg_ready, GB * g + n + 1)
                    nc.vector.scalar_tensor_tensor(out=sg[:, n % 2, :], in0=psum[:, j.slot, :],
                                                   scalar=v("pool_scale", GB * g + n), in1=sg[:, n % 2, :],
                                                   op0=ALU.mult, op1=ALU.mult).then_inc(evacuated[j.slot], 1)

                def mixed(n):
                    j, gj = job(f"M{n}"), job(f"G{n}")
                    dve.wait_ge(evacuated[gj.slot], gj.read)
                    dve.wait_ge(psum_full, j.full)
                    nc.vector.scalar_tensor_tensor(out=sg[:, n % 2, :], in0=psum[:, j.slot, :],
                                                   scalar=v("pool_b", GB * g + n), in1=sg[:, n % 2, :],
                                                   op0=ALU.add, op1=ALU.mult).then_inc(evacuated[j.slot], 1)

                def mixed_lo(n):
                    dve.wait_ge(yhi_ready, 2 * HEADS + GB * g + n + 1)
                    hi, lo = (y_hi, y_lo) if n < 2 else pair_operands(last)[2:]
                    nc.vector.tensor_tensor(lo[:, n % 2, :], sg[:, n % 2, :], hi[:, n % 2, :].bitcast(F32),
                                            ALU.subtract).then_inc(ylo_ready, 1)

                for n in range(GB):
                    split_lo(w_lo[:, n % 2, :], w_hi[:, n % 2, :], unit(("V2", "V3", "G0", "G1")[n]))
                    pool_block(n)
                    queued(2 * n, 2 * n + 1)
                    pool_lo(n)
                split_lo(wo_lo[:, 0, :], wo_hi[:, 0, :], unit("WoA"))
                split_lo(wo_lo[:, 1, :], wo_hi[:, 1, :], unit("WoB"))
                split_lo(w_lo[:, 0, :], w_hi[:, 0, :], unit("M01"))
                gates(0)
                split_lo(w_lo[:, 1, :], w_hi[:, 1, :], unit("G2"))
                gates(1)
                mixed(0)
                split_lo(w_lo[:, 0, :], w_hi[:, 0, :], unit("G3"))
                mixed(1)
                mixed_lo(0)
                mixed_lo(1)
                split_lo(w_lo[:, 1, :], w_hi[:, 1, :], unit("M23"))
                gates(2)
                outs(0, 1, 2, 3)
                gates(3)
                if last:
                    split_lo(w_lo[:, 0, :], w_hi[:, 0, :], unit("WoC"))
                    mixed(2)
                    mixed(3)
                    split_lo(w_lo[:, 1, :], w_hi[:, 1, :], unit("WoD"))
                    outs(4, 5)
                    mixed_lo(2)
                    mixed_lo(3)
                    outs(6, 7)
                    return
                outs(4, 5, 6, 7)
                split_lo(wo_lo[:, 0, :], wo_hi[:, 0, :], unit("WoC"))
                split_lo(wo_lo[:, 1, :], wo_hi[:, 1, :], unit("WoD"))
                split_lo(w_lo[:, 0, :], w_hi[:, 0, :], unit("V0'"))
                mixed(2)
                mixed(3)
                split_lo(w_lo[:, 1, :], w_hi[:, 1, :], unit("V1'"))
                mixed_lo(2)
                mixed_lo(3)

            for g in range(GROUPS):
                l1(g)

            sq, ssq = (sg[:, 0, :], sg[:, 1, :]), vp[:, PAD:]
            for k in range(KB - 1):
                residual(k, 1, Job(J_L1O + k))
                if k:
                    sum_squares(k - 1, 2, sq, ssq)
            last_block(2, Job(J_L1O + KB - 1), sq)
            inverse(2, Job(J_STAT2))
            for b in range(1, SB, 2):
                j = Job(J_OUT + b)
                dve.wait_ge(psum_full, j.full)
                nc.vector.tensor_scalar(ob[:, b, :], psum[:, j.slot, :], rstd[:, 2, b:b + 1], None, ALU.mult)\
                  .then_inc(evacuated[j.slot], 1)

        @block.tensor
        def _(pe):
            def take(job):
                if job.const >= SLOTS or not isinstance(job.turn, int):
                    pe.wait_ge(evacuated[job.slot], job.free)

            def products(dst, whi, wlo, xhi, xlo, first, last):
                for hh in range(NH):
                    cols = slice(hh * HALF, (hh + 1) * HALF)
                    nc.tensor.matmul(dst[:, cols], whi, xhi[:, cols], start=first, stop=False)
                    nc.tensor.matmul(dst[:, cols], whi, xlo[:, cols], start=False, stop=False)
                for hh in range(NH):
                    cols = slice(hh * HALF, (hh + 1) * HALF)
                    ins = nc.tensor.matmul(dst[:, cols], wlo, xhi[:, cols], start=False, stop=last)
                return ins

            def product(job, blocks):
                take(job)
                for n, block in enumerate(blocks):
                    ins = products(psum[:, job.slot, :], *block, n == 0, n == len(blocks) - 1)
                ins.then_inc(psum_full, 1)

            def weights(slot):
                return [(w_hi[:, slot, k * P:(k + 1) * P], w_lo[:, slot, k * P:(k + 1) * P], h_hi[:, k, :],
                         h_lo[:, k, :]) for k in range(KB)]

            def project(job, slot):
                product(job, weights(slot))

            def first_projects(jobs, turn, half, second_unit):
                if half == 0:
                    for job in jobs:
                        take(job)
                    order = [(k, n) for k in range(KB // 2) for n in range(2)]
                else:
                    order = [(4, 0), (4, 1), (5, 0), (6, 0), (5, 1), (7, 0), (6, 1), (7, 1)]
                if (turn, order[0][0]) in FIRST_H:
                    k, order = order[0][0], order[2:]
                    for hh, cols in enumerate(HALVES):
                        pe.wait_ge(h_ready, h_count(turn, k, hh))
                        for n in range(2):
                            if half == 0 and (hh, n) == (0, 1):
                                pe.wait_ge(unit_done, second_unit)
                            whi, wlo, xhi, xlo = weights(n)[k]
                            dst = psum[:, jobs[n].slot, cols]
                            nc.tensor.matmul(dst, whi, xhi[:, cols], start=k == 0, stop=False)
                            nc.tensor.matmul(dst, whi, xlo[:, cols], start=False, stop=False)
                            nc.tensor.matmul(dst, wlo, xhi[:, cols], start=False, stop=False)
                for k, n in order:
                    pe.wait_ge(h_ready, h_count(turn, k))
                    if (k, n) == (0, 1):
                        pe.wait_ge(unit_done, second_unit)
                    ins = products(psum[:, jobs[n].slot, :], *weights(n)[k], k == 0, k == KB - 1)
                    if k == KB - 1:
                        ins.then_inc(psum_full, 1)

            def out_project(job, k, operands=(wo_hi, wo_lo, y_hi, y_lo)):
                whi, wlo, yhi, ylo = operands
                product(job, [(whi[:, m, k * P:(k + 1) * P], wlo[:, m, k * P:(k + 1) * P], yhi[:, m, :], ylo[:, m, :])
                              for m in range(2)])

            def column_sums(job, acc, blocks):
                take(job)
                for n in range(blocks):
                    ins = nc.tensor.matmul(psum[:, job.slot, n:n + 1], acc[:, n * P:(n + 1) * P], ones[:, 0:1],
                                           start=True, stop=True)
                ins.then_inc(psum_full, 1)

            def square_sums(job, turn, last, part):
                if not last:
                    take(job)
                    pe.wait_ge(ssq_added, turn * (KB - 2))
                for b in range(SB):
                    if last and b % (SB // NH) == 0:
                        pe.wait_ge(last_sum, NH * (turn - 1) + b // (SB // NH) + 1)
                    ins = nc.tensor.matmul(psum[:, job.slot, b:b + 1], part[:, b * P:(b + 1) * P], ones[:, 0:1],
                                           start=not last and b == 0, stop=last, skip_group_check=True)
                if last:
                    ins.then_inc(psum_full, 1)

            def broadcast(job, diag, ready):
                take(job)
                for hh in range(NH):
                    pe.wait_ge(ready, (hh + 1) * SB // NH)
                    cols = slice(hh * HALF, (hh + 1) * HALF)
                    nc.tensor.matmul(psum[:, job.slot, cols], ones[:, :], diag[:, cols], start=True, stop=True)\
                      .then_inc(psum_full if hh == NH - 1 else bc_half, 1)

            pe.wait_ge(const_step, CONSTS)
            pe.wait_ge(c_in, 16)
            nc.tensor.transpose(psum[:, J_C, 0:KB], rows_c[:, :], ident[0:KB, 0:KB]).then_inc(psum_full, 1)
            for b in range(SB):
                j = Job(J_XT + b)
                take(j)
                pe.wait_ge(x_in[b], 16)
                for k in range(KB):
                    ins = nc.tensor.transpose(psum[:, j.slot, k * P:(k + 1) * P], x_rows[:, b, k * P:(k + 1) * P],
                                              ident[:, :])
                ins.then_inc(psum_full, 1)
            j = Job(J_VEC)
            take(j)
            pe.wait_ge(rows_in, 16 * (len(ROWS_A) + len(ROWS_B)))
            nc.tensor.transpose(psum[:, j.slot, 0:P], rows_a[:, :], ident[:, :])
            nc.tensor.transpose(psum[:, j.slot, P:NCOL], rows_b[:, :], ident[0:NCOL - P, 0:NCOL - P])\
              .then_inc(psum_full, 1)

            broadcast(Job(J_BC0), diag0, diag0_ready)
            def modulation_sums(half):
                job = Job(J_MOD0 + half)
                parts = [(mod_acc[:, half * D:(half + 1) * D], ones[:, 0:1], *stage_done((half + 1) * KB - 1), psum_full)]
                if half == 0:
                    parts.insert(0, (stage[:, DIRECT % 4, :], ca[:, DIRECT:DIRECT + 1], stage_in[DIRECT % 4],
                                     16 * (DIRECT // 4 + 1), stage_summed))
                take(job)
                for m, (rows, column, ready, value, done) in enumerate(parts):
                    pe.wait_ge(ready, value)
                    for n in range(KB):
                        ins = nc.tensor.matmul(psum[:, job.slot, n:n + 1], rows[:, n * P:(n + 1) * P], column,
                                               start=m == 0 and n == 0, stop=done is psum_full, skip_group_check=True)
                    ins.then_inc(done, 1)

            for half in range(2):
                modulation_sums(half)
                if half == 0:
                    pe.wait_ge(unit_done, 1)
                first_projects((Job(J_L0), Job(J_L0 + 1)), 0, half, 2)

            def l0(i, first):
                for name in (L0_FIRST if first else L0_NEXT):
                    j = l0_job(name, i, first)
                    if name[0] == "O":
                        k = int(name[1])
                        if k == 0:
                            pe.wait_ge(ylo_ready, 2 * i)
                            pe.wait_ge(unit_done, l0_unit("WoB", i - 1)[3])
                        out_project(j, k)
                    elif name == "GM":
                        pe.wait_ge(*stage_done(3 * KB - 1))
                        column_sums(j, gate_acc, KB)
                    elif name in ("r", "i"):
                        if name == "r":
                            pe.wait_ge(xc_ready, i + 1)
                            pe.wait_ge(unit_done, l0_unit("G", i)[3])
                        at = slice(0, P) if name == "r" else slice(P, 2 * P)
                        product(j, [(g_hi[:, at], g_lo[:, at], xc_hi[:, :], xc_lo[:, :])])
                    else:
                        slot = ("xa", "gc", "v", "ga", "gbp", "gb").index(name) % 2
                        if name not in ("xa", "gc"):
                            pe.wait_ge(unit_done, l0_unit(name, i)[3])
                        elif first:
                            continue
                        else:
                            pe.wait_ge(unit_done, l0_unit(name + "'", i - 1)[3])
                        project(j, slot)

            l0(0, True)
            with pe.Fori(1, HEADS) as i:
                l0(i, False)
            pe.wait_ge(unit_done, l0_unit("M2", HEADS - 1)[3])
            column_sums(Job(J_MOD1), mod_acc, 2 * KB)
            pe.wait_ge(ylo_ready, 2 * HEADS)
            pe.wait_ge(unit_done, l0_unit("WoB", HEADS - 1)[3])
            for k in range(KB):
                out_project(Job(J_L0O + k), k)
            square_sums(Job(J_STAT1), 1, False, scr[:, 2, :])
            square_sums(Job(J_STAT1), 1, True, scr[:, 0, :])
            column_sums(Job(J_GATE1), mod_acc[:, 2 * D:3 * D], KB)
            broadcast(Job(J_BC1), scr[:, 3, :], diag_ready)

            def l1(g, first, last):
                for name in (L1_FIRST if first else L1_LAST if last else L1_NEXT):
                    j = l1_job(name, g, first, last)
                    n = int(name[1])
                    if name[0] in "QO":
                        if n == 0 and name[0] == "Q":
                            pe.wait_ge(ylo_ready, GB * g + 2 * HEADS)
                            pe.wait_ge(unit_done, l1_unit("WoD", g - 1)[3])
                        elif n == 0:
                            pe.wait_ge(ylo_ready, GB * g + (2 * HEADS + 2))
                            pe.wait_ge(unit_done, l1_unit("WoB", g)[3])
                        out_project(j, n)
                    elif name[0] == "M":
                        if n == 0:
                            pe.wait_ge(dlo_ready, GB * g + GB)
                        pe.wait_ge(unit_done, l1_unit("M01" if n < 2 else "M23", g)[3])
                        slot, cols = n // 2, (n % 2) * P
                        product(j, [(w_hi[:, slot, k * 2 * P + cols:k * 2 * P + cols + P],
                                     w_lo[:, slot, k * 2 * P + cols:k * 2 * P + cols + P], d_hi[:, k, :], d_lo[:, k, :])
                                    for k in range(GB)])
                    else:
                        slot = {"V0": 0, "V1": 1, "V2": 0, "V3": 1, "G0": 0, "G1": 1, "G2": 1, "G3": 0}[name]
                        if name not in ("V0", "V1"):
                            pe.wait_ge(unit_done, l1_unit(name, g)[3])
                        elif first:
                            if n:
                                pe.wait_ge(unit_done, l0_unit("xa'", HEADS - 1)[3])
                                for half in range(2):
                                    first_projects((Job(J_L1), Job(J_L1 + 1)), 1, half,
                                                   l0_unit("gc'", HEADS - 1)[3])
                            continue
                        else:
                            pe.wait_ge(unit_done, l1_unit(name + "'", g - 1)[3])
                        project(j, slot)

            l1(0, True, False)
            with pe.Fori(1, GROUPS - 1) as g:
                l1(g, False, False)
            l1(GROUPS - 1, False, True)
            pe.wait_ge(ylo_ready, 2 * HEADS + GB * GROUPS)
            pe.wait_ge(unit_done, l1_unit("WoD", GROUPS - 1)[3])
            for k in range(KB):
                out_project(Job(J_L1O + k), k, pair_operands(True))
            def to_rows(b, blocks):
                j = Job(J_OUT + b)
                if 0 in blocks:
                    take(j)
                for k in blocks:
                    ins = nc.tensor.transpose(psum[:, j.slot, k * P:(k + 1) * P], xT[:, k, b * P:(b + 1) * P],
                                              ident[:, :])
                if KB - 1 in blocks:
                    ins.then_inc(psum_full, 1)

            early, late = range(KB - 2), range(KB - 2, KB)
            square_sums(Job(J_STAT2), 2, False, vp[:, PAD:])
            pe.wait_ge(xg_ready, KB - 2)
            to_rows(0, early)
            to_rows(1, early)
            square_sums(Job(J_STAT2), 2, True, sg[:, 0, :])
            pe.wait_ge(xg_ready, KB)
            to_rows(0, late)
            to_rows(1, late)
            for b in range(2, SB):
                to_rows(b, range(KB))


_INS = ["x", "c", "norm_g", "mod_w", "mod_b", "hy_w_in", "hy_conv_w", "hy_conv_b", "lru_w_a", "lru_b_a", "lru_w_x",
        "lru_b_x", "lru_lambda", "sc_conv_w", "hy_w_out", "pool_w_in", "pool_w_grp", "pool_b_grp", "pool_scale",
        "pool_w_out", "final_g"]


def kernel(**inputs):
    import numpy as np
    import concourse.bacc as bacc
    from concourse.bass_utils import run_bass_kernel_spmd

    nc = bacc.Bacc("TRN2", target_bir_lowering=False, num_devices=1, dynamic_dma_scratch_size=512)
    arrays, args = {}, []
    for name in _INS:
        a = np.ascontiguousarray(inputs[name])
        arrays[f"in_{name}"] = a
        args.append(nc.dram_tensor(f"in_{name}", a.shape, mybir.dt.from_np(a.dtype), kind="ExternalInput").ap())
    out = nc.dram_tensor("out", arrays["in_x"].shape, F32, kind="ExternalOutput").ap()
    build(nc, *args, out)
    r = run_bass_kernel_spmd(nc, [arrays], core_ids=[0])
    return r.results[0]["out"]
```
